# Optimizing a Trainium2 kernel written in Bass

```python
import math
import jax
import jax.numpy as jnp
from jax import lax
import numpy as np

D_MODEL = 1024
BATCH = 1
SEQ = 256
DEPTH = 2

GRID_W = 64
CTX_LEN = 256
HEAD_DIM = 64
NA_HEADS = 6
NA_WIN_H = 8
NA_WIN_W = 16
DIFF_HEADS = 4
DIFF_QK_DIM = 32
DIFF_V_DIM = 2 * DIFF_QK_DIM
GQA_Q_HEADS = 6
GQA_KV_HEADS = 2
GQA_GROUP = GQA_Q_HEADS // GQA_KV_HEADS
N_GROUPS = 4
EXPERTS_PER_GROUP = 4
N_EXPERTS = N_GROUPS * EXPERTS_PER_GROUP
TOP_K_IN_GROUP = 2
EXPERT_HIDDEN = 512
Q_BLOCK = 128
ROPE_THETA = 10000.0
EPS = 1e-6
W_A = NA_HEADS * HEAD_DIM
W_B = DIFF_HEADS * DIFF_V_DIM
W_C = GQA_Q_HEADS * HEAD_DIM
MIX_WIDTH = W_A + W_B + W_C
PROJ_SIZES = (W_A, W_A, W_A, 2 * DIFF_HEADS * DIFF_QK_DIM, 2 * DIFF_HEADS * DIFF_QK_DIM, W_B, W_C, GQA_KV_HEADS * HEAD_DIM, GQA_KV_HEADS * HEAD_DIM)
IN_WIDTH = sum(PROJ_SIZES)

kernel_name = 'hybrid_na_diff_gqa_hmoe_block'

def rms_norm(x, g):
    xf = x.astype(jnp.float32)
    y = xf * lax.rsqrt(jnp.mean(xf * xf, axis=-1, keepdims=True) + EPS)
    return (y * g.astype(jnp.float32)).astype(x.dtype)

def split_proj(p):
    outs, start = [], 0
    for w in PROJ_SIZES:
        outs.append(p[..., start:start + w])
        start += w
    return outs

def split_heads(t, n):
    b, s, w = t.shape
    return t.reshape(b, s, n, w // n).transpose(0, 2, 1, 3)

def merge_heads(t):
    b, h, s, d = t.shape
    return t.transpose(0, 2, 1, 3).reshape(b, s, h * d)

def diff_split(t):
    b, s, _ = t.shape
    t = t.reshape(b, s, DIFF_HEADS, 2, DIFF_QK_DIM).transpose(3, 0, 2, 1, 4)
    return t[0], t[1]

def axial_rope(n_tokens, dim):
    t = jnp.arange(n_tokens)
    row = (t // GRID_W).astype(jnp.float32)
    col = (t % GRID_W).astype(jnp.float32)
    quarter = dim // 4
    freqs = ROPE_THETA ** (-jnp.arange(quarter, dtype=jnp.float32) / quarter)
    ang = jnp.concatenate([row[:, None] * freqs, col[:, None] * freqs], axis=-1)
    return jnp.cos(ang), jnp.sin(ang)

def apply_rope(x, cos, sin):
    half = x.shape[-1] // 2
    xf = x.astype(jnp.float32)
    x1, x2 = xf[..., :half], xf[..., half:]
    return jnp.concatenate([x1 * cos - x2 * sin, x2 * cos + x1 * sin], axis=-1).astype(x.dtype)

def to_blocks(t):
    *lead, s, d = t.shape
    return jnp.moveaxis(t.reshape(*lead, s // Q_BLOCK, Q_BLOCK, d), -3, 0)

def from_blocks(t):
    t = jnp.moveaxis(t, 0, -3)
    *lead, nb, q, d = t.shape
    return t.reshape(*lead, nb * q, d)

def softmax_attend(q, k, v):
    logits = jnp.einsum('bhqd,bhkd->bhqk', q, k).astype(jnp.float32) * (q.shape[-1] ** -0.5)
    p = jax.nn.softmax(logits, axis=-1)
    return jnp.einsum('bhqk,bhkd->bhqd', p.astype(v.dtype), v)

def diff_attend(q1, q2, k1, k2, v, lam):
    scale = DIFF_QK_DIM ** -0.5
    p1 = jax.nn.softmax(jnp.einsum('bhqd,bhkd->bhqk', q1, k1).astype(jnp.float32) * scale, axis=-1)
    p2 = jax.nn.softmax(jnp.einsum('bhqd,bhkd->bhqk', q2, k2).astype(jnp.float32) * scale, axis=-1)
    a = p1 - lam * p2
    return jnp.einsum('bhqk,bhkd->bhqd', a.astype(v.dtype), v)

def gqa_attend(q, k, v):
    logits = jnp.einsum('bgrqd,bgkd->bgrqk', q, k).astype(jnp.float32) * (HEAD_DIM ** -0.5)
    p = jax.nn.softmax(logits, axis=-1)
    return jnp.einsum('bgrqk,bgkd->bgrqd', p.astype(v.dtype), v)

def neighbourhood_attention(q, k, v, k_ctx, v_ctx, rpb):
    b, h, s, d = q.shape
    rows = s // GRID_W
    kh = min(NA_WIN_H, rows)
    kw = NA_WIN_W
    qg = q.reshape(b, h, rows, GRID_W, d)
    kg = k.reshape(b, h, rows, GRID_W, d)
    vg = v.reshape(b, h, rows, GRID_W, d)
    cols = jnp.arange(GRID_W)
    col_idx = jnp.clip(cols - kw // 2, 0, GRID_W - kw)[:, None] + jnp.arange(kw)[None, :]
    dc = col_idx - cols[:, None] + (NA_WIN_W - 1)
    scale = d ** -0.5
    rpb32 = rpb.astype(jnp.float32)

    def row_block(r):
        r0 = jnp.clip(r - kh // 2, 0, rows - kh)
        k_rows = lax.dynamic_slice_in_dim(kg, r0, kh, axis=2)
        v_rows = lax.dynamic_slice_in_dim(vg, r0, kh, axis=2)
        k_win = k_rows[:, :, :, col_idx, :]
        v_win = v_rows[:, :, :, col_idx, :]
        q_r = lax.dynamic_index_in_dim(qg, r, axis=2, keepdims=False)
        dr = r0 + jnp.arange(kh) - r + (NA_WIN_H - 1)
        bias = rpb32[:, dr[:, None, None], dc[None, :, :]].transpose(0, 2, 1, 3)
        s_win = jnp.einsum('bhcd,bhicjd->bhcij', q_r, k_win).astype(jnp.float32) * scale + bias[None]
        s_ctx = jnp.einsum('bhcd,bhld->bhcl', q_r, k_ctx).astype(jnp.float32) * scale
        logits = jnp.concatenate([s_win.reshape(b, h, GRID_W, kh * kw), s_ctx], axis=-1)
        p = jax.nn.softmax(logits, axis=-1).astype(v.dtype)
        p_win = p[..., :kh * kw].reshape(b, h, GRID_W, kh, kw)
        return (jnp.einsum('bhcij,bhicjd->bhcd', p_win, v_win)
                + jnp.einsum('bhcl,bhld->bhcd', p[..., kh * kw:], v_ctx))

    out = lax.map(row_block, jnp.arange(rows))
    return out.transpose(1, 2, 0, 3, 4).reshape(b, h, s, d)

def token_mixers(h, hc, w_in, na_rpb, lq1, lk1, lq2, lk2, diff_subln, q_norm, k_norm, lam_init, ctx_out):
    b, s, _ = h.shape
    n_ctx = hc.shape[1]
    qa, ka, va, qb, kb, vb, qc, kc, vc = split_proj(h @ w_in)
    qa_c, ka_c, va_c, qb_c, kb_c, vb_c, qc_c, kc_c, vc_c = split_proj(hc @ w_in)
    cos_b, sin_b = axial_rope(s, DIFF_QK_DIM)
    cos_c, sin_c = axial_rope(s, HEAD_DIM)

    ka_ctx, va_ctx = split_heads(ka_c, NA_HEADS), split_heads(va_c, NA_HEADS)
    out_a = neighbourhood_attention(split_heads(qa, NA_HEADS), split_heads(ka, NA_HEADS),
                                    split_heads(va, NA_HEADS), ka_ctx, va_ctx, na_rpb)

    lam = (jnp.exp(jnp.sum(lq1.astype(jnp.float32) * lk1.astype(jnp.float32)))
           - jnp.exp(jnp.sum(lq2.astype(jnp.float32) * lk2.astype(jnp.float32))) + lam_init)
    q1, q2 = diff_split(qb)
    k1, k2 = diff_split(kb)
    k1c, k2c = diff_split(kb_c)
    vb_lat, vb_ctx = split_heads(vb, DIFF_HEADS), split_heads(vb_c, DIFF_HEADS)
    q1, q2, k1, k2 = [apply_rope(t, cos_b, sin_b) for t in (q1, q2, k1, k2)]
    k1_all = jnp.concatenate([k1c, k1], axis=2)
    k2_all = jnp.concatenate([k2c, k2], axis=2)
    vb_all = jnp.concatenate([vb_ctx, vb_lat], axis=2)
    out_b = from_blocks(lax.map(lambda qq: diff_attend(qq[0], qq[1], k1_all, k2_all, vb_all, lam),
                                (to_blocks(q1), to_blocks(q2))))
    out_b = rms_norm(out_b, diff_subln) * (1.0 - lam_init)

    q = apply_rope(rms_norm(split_heads(qc, GQA_Q_HEADS), q_norm), cos_c, sin_c)
    k = apply_rope(rms_norm(split_heads(kc, GQA_KV_HEADS), k_norm), cos_c, sin_c)
    kc_ctx = rms_norm(split_heads(kc_c, GQA_KV_HEADS), k_norm)
    vc_ctx = split_heads(vc_c, GQA_KV_HEADS)
    kc_all = jnp.concatenate([kc_ctx, k], axis=2)
    vc_all = jnp.concatenate([vc_ctx, split_heads(vc, GQA_KV_HEADS)], axis=2)
    qg = q.reshape(b, GQA_KV_HEADS, GQA_GROUP, s, HEAD_DIM)
    out_c = from_blocks(lax.map(lambda qq: gqa_attend(qq, kc_all, vc_all), to_blocks(qg)))
    out_c = out_c.reshape(b, GQA_Q_HEADS, s, HEAD_DIM)

    mixed = jnp.concatenate([merge_heads(out_a), merge_heads(out_b), merge_heads(out_c)], axis=-1)
    if not ctx_out:
        return mixed, None

    oa_c = softmax_attend(split_heads(qa_c, NA_HEADS), ka_ctx, va_ctx)
    q1c, q2c = diff_split(qb_c)
    ob_c = rms_norm(diff_attend(q1c, q2c, k1c, k2c, vb_ctx, lam), diff_subln) * (1.0 - lam_init)
    qg_c = rms_norm(split_heads(qc_c, GQA_Q_HEADS), q_norm).reshape(b, GQA_KV_HEADS, GQA_GROUP, n_ctx, HEAD_DIM)
    oc_c = gqa_attend(qg_c, kc_ctx, vc_ctx).reshape(b, GQA_Q_HEADS, n_ctx, HEAD_DIM)
    mixed_c = jnp.concatenate([merge_heads(oa_c), merge_heads(ob_c), merge_heads(oc_c)], axis=-1)
    return mixed, mixed_c

def hier_moe(h, wr_g, br_g, wr_e, br_e, w_gate, w_up, w_down):
    n = h.shape[0]
    g_logits = (h @ wr_g).astype(jnp.float32) + br_g.astype(jnp.float32)
    g_sel = jnp.argmax(g_logits, axis=-1)
    p_grp = jnp.take_along_axis(jax.nn.softmax(g_logits, axis=-1), g_sel[:, None], axis=-1)
    e_logits = ((h @ wr_e).astype(jnp.float32) + br_e.astype(jnp.float32)).reshape(n, N_GROUPS, EXPERTS_PER_GROUP)
    e_in = jnp.take_along_axis(e_logits, g_sel[:, None, None], axis=1)[:, 0]
    top_val, top_idx = lax.top_k(e_in, TOP_K_IN_GROUP)
    w_top = jax.nn.softmax(top_val, axis=-1) * p_grp
    expert_id = g_sel[:, None] * EXPERTS_PER_GROUP + top_idx
    combine = jnp.sum(jax.nn.one_hot(expert_id, N_EXPERTS, dtype=jnp.float32) * w_top[..., None], axis=1)
    y = jnp.zeros_like(h)
    for e in range(N_EXPERTS):
        hid = jax.nn.silu(h @ w_gate[e]) * (h @ w_up[e])
        y = y + (hid @ w_down[e]) * combine[:, e:e + 1].astype(h.dtype)
    return y

def setup_inputs(seed: int = 0) -> dict:
    key = jax.random.key(seed)
    ks = jax.random.split(key, 26)
    f32 = jnp.float32
    D = D_MODEL

    def nrm(k, shape, s):
        return jax.random.normal(k, shape, f32) * s

    return {
        'x': nrm(ks[0], (BATCH, SEQ, D), 1.0),
        'c': nrm(ks[1], (BATCH, D), 1.0),
        'ctx': nrm(ks[2], (BATCH, CTX_LEN, D), 1.0),
        'c_ctx': nrm(ks[3], (D,), 1.0),
        'w_mod': nrm(ks[4], (DEPTH, D, 6 * D), 0.5 * D ** -0.5),
        'b_mod': nrm(ks[5], (DEPTH, 6 * D), 0.02),
        'norm_attn': 1.0 + nrm(ks[6], (DEPTH, D), 0.05),
        'norm_ffn': 1.0 + nrm(ks[7], (DEPTH, D), 0.05),
        'w_in': nrm(ks[8], (DEPTH, D, IN_WIDTH), D ** -0.5),
        'w_out': nrm(ks[9], (DEPTH, MIX_WIDTH, D), MIX_WIDTH ** -0.5),
        'na_rpb': nrm(ks[10], (DEPTH, NA_HEADS, 2 * NA_WIN_H - 1, 2 * NA_WIN_W - 1), 0.02),
        'diff_lambda_q1': nrm(ks[11], (DEPTH, DIFF_QK_DIM), 0.1),
        'diff_lambda_k1': nrm(ks[12], (DEPTH, DIFF_QK_DIM), 0.1),
        'diff_lambda_q2': nrm(ks[13], (DEPTH, DIFF_QK_DIM), 0.1),
        'diff_lambda_k2': nrm(ks[14], (DEPTH, DIFF_QK_DIM), 0.1),
        'diff_subln': 1.0 + nrm(ks[15], (DEPTH, DIFF_V_DIM), 0.05),
        'gqa_q_norm': 1.0 + nrm(ks[16], (DEPTH, HEAD_DIM), 0.05),
        'gqa_k_norm': 1.0 + nrm(ks[17], (DEPTH, HEAD_DIM), 0.05),
        'router_group_w': nrm(ks[18], (DEPTH, D, N_GROUPS), D ** -0.5),
        'router_group_b': nrm(ks[19], (DEPTH, N_GROUPS), 0.01),
        'router_expert_w': nrm(ks[20], (DEPTH, D, N_EXPERTS), D ** -0.5),
        'router_expert_b': nrm(ks[21], (DEPTH, N_EXPERTS), 0.01),
        'w_gate': nrm(ks[22], (DEPTH, N_EXPERTS, D, EXPERT_HIDDEN), D ** -0.5),
        'w_up': nrm(ks[23], (DEPTH, N_EXPERTS, D, EXPERT_HIDDEN), D ** -0.5),
        'w_down': nrm(ks[24], (DEPTH, N_EXPERTS, EXPERT_HIDDEN, D), EXPERT_HIDDEN ** -0.5),
        'final_norm': 1.0 + nrm(ks[25], (D,), 0.05),
    }

def reference(x, c, ctx, c_ctx, w_mod, b_mod, norm_attn, norm_ffn, w_in, w_out, na_rpb,
              diff_lambda_q1, diff_lambda_k1, diff_lambda_q2, diff_lambda_k2, diff_subln,
              gqa_q_norm, gqa_k_norm, router_group_w, router_group_b, router_expert_w,
              router_expert_b, w_gate, w_up, w_down, final_norm):
    b, s, d = x.shape
    n_ctx = ctx.shape[1]
    xc = ctx
    for l in range(DEPTH):
        ctx_out = l < DEPTH - 1
        lam_init = 0.8 - 0.6 * math.exp(-0.3 * l)
        mod = jax.nn.silu(c) @ w_mod[l] + b_mod[l]
        mod_c = jax.nn.silu(c_ctx) @ w_mod[l] + b_mod[l]
        sh1, sc1, g1, sh2, sc2, g2 = jnp.split(mod[:, None, :], 6, axis=-1)
        csh1, csc1, cg1, csh2, csc2, cg2 = jnp.split(mod_c, 6, axis=-1)
        h = rms_norm(x, norm_attn[l]) * (1.0 + sc1) + sh1
        hc = rms_norm(xc, norm_attn[l]) * (1.0 + csc1) + csh1
        mixed, mixed_c = token_mixers(h, hc, w_in[l], na_rpb[l], diff_lambda_q1[l], diff_lambda_k1[l],
                                      diff_lambda_q2[l], diff_lambda_k2[l], diff_subln[l],
                                      gqa_q_norm[l], gqa_k_norm[l], lam_init, ctx_out)
        x = x + g1 * (mixed @ w_out[l])
        tokens = (rms_norm(x, norm_ffn[l]) * (1.0 + sc2) + sh2).reshape(b * s, d)
        if ctx_out:
            xc = xc + cg1 * (mixed_c @ w_out[l])
            hfc = rms_norm(xc, norm_ffn[l]) * (1.0 + csc2) + csh2
            tokens = jnp.concatenate([tokens, hfc.reshape(b * n_ctx, d)], axis=0)
        y = hier_moe(tokens, router_group_w[l], router_group_b[l], router_expert_w[l], router_expert_b[l],
                     w_gate[l], w_up[l], w_down[l])
        x = x + g2 * y[:b * s].reshape(b, s, d)
        if ctx_out:
            xc = xc + cg2 * y[b * s:].reshape(b, n_ctx, d)
    return rms_norm(x, final_norm)


_drawn_inputs = setup_inputs


def setup_inputs(seed=0):
    import zlib

    import numpy as np

    out = dict(_drawn_inputs(seed))
    spreads = {}
    factors = {'norm_attn': 4.338,
     'na_rpb': 8.0,
     'diff_lambda_q1': 3.94,
     'diff_lambda_k1': 5.559,
     'diff_lambda_q2': 6.918,
     'diff_lambda_k2': 8.0,
     'diff_subln': 4.478,
     'gqa_q_norm': 8.0,
     'gqa_k_norm': 8.0,
     'router_group_b': 8.0,
     'router_expert_b': 8.0}
    for name, (base, spread) in spreads.items():
        noise = np.random.default_rng([zlib.crc32(name.encode()), seed]).standard_normal(out[name].shape)
        drawn = base * np.exp(spread * noise) if base else spread * noise
        out[name] = jnp.asarray(drawn.astype(out[name].dtype))
    for name, factor in factors.items():
        out[name] = (out[name] * factor).astype(out[name].dtype)
    return out
```

```python
import math
from contextlib import ExitStack

import numpy as np

import concourse.bass as bass
from concourse import mybir

P = 128
F32 = mybir.dt.float32
I32 = mybir.dt.int32
ALU = mybir.AluOpType
ACT = mybir.ActivationFunctionType
AX = mybir.AxisListType

D = 1024
KD = D // P
SEQ = 256
CTX = 256
GRID_W = 64
LAYERS = 2
IN_W = 2560
HID = 512
N_EXP = 16
N_GRP = 4
N_TOK = SEQ + CTX
TILES = N_TOK // P
XT = SEQ // P
EPS = 1e-6
BIG = 1e30
BLOCK = 64
SLOTS = 6
SLOT_W = 4096
HG_AHEAD = 4
Y_BUFS = 4
MAX_BLOCKS = 2 * N_TOK // BLOCK + N_EXP

C_ID, C_TRI, C_ONE, C_IG, C_IE, C_THR, C_C16, C_S16, C_C32, C_S32, C_MASK, C_FLIP, C_END = np.cumsum(
    [0, P, P, 1, N_GRP, N_EXP, 7, 64, 64, 128, 128, 64, P]).tolist()


def constant_table():
    t = np.zeros((P, C_END), np.float32)
    t[:, C_ID:C_ID + P] = np.eye(P)
    t[:, C_TRI:C_TRI + P] = np.triu(np.ones((P, P)), 1)
    t[:, C_ONE] = 1.0
    t[:, C_IG:C_IG + N_GRP] = np.arange(N_GRP) - N_GRP
    t[:, C_IE:C_IE + N_EXP] = np.arange(N_EXP) - N_EXP
    t[:, C_THR:C_THR + 7] = BLOCK * np.arange(1, 8)
    for dim, cc, ss in ((32, C_C16, C_S16), (64, C_C32, C_S32)):
        tok = np.arange(SEQ)
        freqs = (np.float32(10000.0) ** (-np.arange(dim // 4, dtype=np.float32) / np.float32(dim // 4)))
        ang = np.concatenate([(tok // GRID_W).astype(np.float32)[:, None] * freqs,
                              (tok % GRID_W).astype(np.float32)[:, None] * freqs], -1)
        cos, sin = np.cos(ang), np.sin(ang)
        for i in range(XT):
            rows = slice(i * P, (i + 1) * P)
            t[:, cc + dim * i:cc + dim * (i + 1)] = np.concatenate([cos[rows], cos[rows]], -1)
            t[:, ss + dim * i:ss + dim * (i + 1)] = np.concatenate([-sin[rows], sin[rows]], -1)
    col = np.arange(GRID_W)
    start = np.clip(col - 8, 0, GRID_W - 16)[:, None]
    inside = (col[None] >= start) & (col[None] < start + 16)
    t[:, C_MASK:C_MASK + 64] = np.tile(np.where(inside, 0.0, -BIG)[::-1], (2, 1))
    t[:, C_FLIP:C_FLIP + P] = np.kron(np.eye(2), np.eye(GRID_W)[::-1])
    return t


GROUPS = {"F": [(1920, 2432)], "D": [(1152, 1664)], "A": [(0, 384)], "B": [(384, 768)], "C": [(768, 1152)],
          "E": [(1664, 1920), (2432, 2560)]}


def query_tiles(l):
    return TILES if l < LAYERS - 1 else XT


def head_units(l):
    sides = (True, False) if l < LAYERS - 1 else (True,)
    return [(k, h, x) for k, n in (("na", 6), ("diff", 4), ("gqa", 6)) for h in range(n) for x in sides]


def in_products(l):
    out = [("F", l, t) for t in range(TILES)] + [("D", l, t) for t in range(TILES)]
    out += [("Ft", l, t) for t in range(TILES)] + [("A", l, m) for m in range(3)]
    out += [("Dt", l, t) for t in range(TILES)] + [("B", l, m) for m in range(3)]
    out += [("C", l, t) for t in range(TILES)] + [("E", l, t) for t in range(TILES)]
    return out


MOD_LATER = [(0, r, k) for r in (1, 2) for k in range(4)] + [(1, r, k) for r in range(3) for k in range(4)]


def mod_pieces_after(place):
    kind, n = place
    if kind == "in":
        ks = [i for i, p in enumerate(in_products(0)) if p[0] in "DABCE" and len(p[0]) == 1][::2]
        i = ks.index(n) if n in ks else None
    else:
        i = 9 + n // 3 if n % 3 == 0 else None
    return [] if i is None or i >= len(MOD_LATER) else [MOD_LATER[i]]


def psum_products():
    order = []
    turn = [0]

    def rotate(key):
        order.append((key, turn[0] % 6))
        turn[0] += 1

    def mods(place):
        for l, r, k in mod_pieces_after(place):
            if k == 3:
                order.append((("mod", l, r), 7))

    order.append((("mod", 0, 0), 7))
    for l in range(LAYERS):
        for t in range(TILES):
            for half in range(2):
                rotate(("tr1", l, t, half))
        for n, key in enumerate(in_products(l)):
            rotate(key)
            if l == 0:
                mods(("in", n))
        units = head_units(l)

        def scores(u):
            kind, h, x = units[u]
            if kind == "diff":
                sets = [(0, 0), (1, 2)]
            else:
                sets = [(0, 2 * (u % 2))]
            for s, b in sets:
                for q in range(2 if x else 1):
                    order.append((("S", l, u, s, q), b + q))

        scores(0)
        for u in range(len(units) + 1):
            if u + 1 < len(units):
                scores(u + 1)
            if u < len(units):
                if units[u][2]:
                    order.append((("T", l, u, 0), 4))
                    order.append((("T", l, u, 1), 5))
                else:
                    order.append((("T", l, u, 0), 4 + u % 2))
            if u >= 1:
                order.append((("O", l, u - 1), 6))
            if l == 0:
                mods(("unit", u))
        turn[0] = 0
        for t in range(query_tiles(l)):
            rotate(("OBt", l, t))
        for t in range(query_tiles(l) + 1):
            if t < query_tiles(l):
                for half in range(2):
                    rotate(("Y", l, t, half))
            if t >= 1:
                for half in range(2):
                    rotate(("tr2", l, t - 1, half))
        order.append((("R", l), 6))
        order.append((("Rt", l), 7))
        order.append((("cum", l), 6))
        turn[0] = 0
    place, count = {}, [0] * 8
    last = {}
    before = {}
    for key, b in order:
        place[key] = (b, count[b])
        count[b] += 1
        before[key] = last.get(b)
        last[b] = key
    return place, before, [k for k, _ in order]


PLACE, BEFORE, ORDER = psum_products()


def ring_plan():
    items = [("mod", 0, 0, k) for k in range(4)]
    for l in range(LAYERS):
        seen = set()
        for n, p in enumerate(in_products(l)):
            if p[0] in GROUPS and p[0] not in seen:
                seen.add(p[0])
                items.append(("in", l, p[0]))
            if l == 0:
                items += [("mod", *m) for m in mod_pieces_after(("in", n))]
        if l == 0:
            for u in range(len(head_units(0)) + 1):
                items += [("mod", *m) for m in mod_pieces_after(("unit", u))]
        items += [("out", l, 0), ("out", l, 1), ("exp", l)]
    plan, n = [], 0
    for it in items:
        plan.append((it, n % SLOTS))
        n += 3 * N_EXP if it[0] == "exp" else 1
    return plan


RING = ring_plan()


def hybrid_block(nc, io, out):
    place, before = PLACE, BEFORE
    with ExitStack() as ctx:
        def sb(name, shape, dt=F32):
            return ctx.enter_context(nc.sbuf_tensor(name, shape, dt))

        def sem(name):
            return ctx.enter_context(nc.semaphore(name))

        def sems(name):
            return [sem(f"{name}_{l}") for l in range(LAYERS)]

        ring = sb("ring", [P, SLOTS, SLOT_W])
        x_res = sb("x_res", [P, TILES, D])
        h_tok = sb("h_tok", [P, TILES, D])
        h_t = sb("h_t", [P, KD, N_TOK])
        rows = sb("rows", [P, 4, D])
        big = sb("big", [P, 10240])
        cst = sb("cst", [P, C_END])
        gains = sb("gains", [P, LAYERS, 2, 64])
        subg = sb("subg", [P, LAYERS, 64])
        rbias = sb("rbias", [P, LAYERS, N_GRP + N_EXP])
        zeros = sb("zeros", [P, 256])
        cond = sb("cond", [P, KD, 2])
        csil = sb("csil", [P, KD, 16, 2])
        stat = sb("stat", [P, 80])
        fstat = sb("fstat", [P, 3, 8])
        neglam = sb("neglam", [P, LAYERS])

        ident = cst[:, C_ID:C_ID + P]
        bank = [ctx.enter_context(nc.psum_tensor(f"bank{i}", [P, 512], F32)) for i in range(8)]

        qk = big[:, 0:7168].rearrange("p (c t) -> p c t", t=N_TOK)
        Q_NA, K_NA, Q_DF, K_DF, Q_GQ, K_GQ = 0, 3, 6, 8, 10, 13
        v_tok = big[:, 7168:10240].rearrange("p (t c) -> p t c", t=TILES)
        ob = big[:, 0:1024].rearrange("p (t c) -> p t c", t=TILES)
        ob_sq = big[:, 1024:2048]
        win = rows[:, 0:3, :].rearrange("p a b -> p (a b)").rearrange("p (q r h c) -> p q r h c", q=2, r=4, h=6)
        mod_row = rows[:, 3, 0:512]
        mod_add = rows[:, 3, 512:1024]
        prob = [h_tok[:, i, :].rearrange("p (q k) -> p q k", q=2) for i in range(2)]
        prob_t = [h_tok[:, 2 + i, :].rearrange("p (k q) -> p k q", k=4) for i in range(2)]
        mixed = h_t

        o = 0

        def carve(n):
            nonlocal o
            o += n
            return big[:, o - n:o]

        w_route = carve(KD * 20).rearrange("p (k n) -> p k n", k=KD)
        y_in = [[carve(1024) for _ in range(2)] for _ in range(2)]
        hg_ring = big[:, o - HG_AHEAD * D:o]
        hg = carve(1024)
        hgt = carve(512).rearrange("p (k r) -> p k r", k=KD)
        sg = carve(512)
        hid = carve(512)
        hidt = carve(256).rearrange("p (k r) -> p k r", k=4)
        y_ring = carve(Y_BUFS * 512)
        lgt_t = y_ring[:, 0:512]
        lg = carve(80)
        rt = carve(1008)
        next_rows = big[:, 2048:4096].rearrange("p (a d) -> p a d", a=2)
        route_i = sb("route_i", [P, 2 * TILES], I32)
        counts_i = sb("counts_i", [P, 2 * N_EXP + 1], I32)
        wsel = sb("wsel", [P, 2, TILES])

        modd = nc.dram_tensor("modd", [LAYERS, 2, 6 * D], F32).ap()
        wind = nc.dram_tensor("wind", [LAYERS, 15, 6, 128], F32).ap()
        hbuf = nc.dram_tensor("hbuf", [(MAX_BLOCKS + HG_AHEAD) * BLOCK, D], F32).ap()

        bank_full = [sem(f"bank_full{b}") for b in range(8)]
        bank_read = [sem(f"bank_read{b}") for b in range(8)]
        slot_in = [sem(f"slot_in{s}") for s in range(SLOTS)]
        mod_piece = sem("mod_piece")
        consts_in = sem("consts_in")
        cond_in = sem("cond_in")
        x_in = sem("x_in")
        csil_ready = sem("csil_ready")
        zeroed = sem("zeroed")
        wind_zero = sem("wind_zero")
        wind_in = sem("wind_in")
        hbuf_zero = sem("hbuf_zero")
        dve_order = sem("dve_order")
        act_order = sem("act_order")
        lam_dots = sem("lam_dots")
        lam_exp = sem("lam_exp")
        mod_b_in = sem("mod_b_in")
        mod_sum = sem("mod_sum")
        mod_done = sem("mod_done")
        mod_stored = sem("mod_stored")
        ga_in = [sems(f"rows{i}_in") for i in range(3)]
        ssq = sems("ssq")
        var = sems("var")
        std = sems("std")
        h_ready = sems("h_ready")
        fsq = sems("fsq")
        fvar = sems("fvar")
        fstd = sems("fstd")
        rope_ready = sems("rope_ready")
        ctx_copied = sems("ctx_copied")
        win_ready = sems("win_ready")
        max_ready = sems("max_ready")
        exp_ready = sems("exp_ready")
        probs_ready = sems("probs_ready")
        sub_var = sems("sub_var")
        sub_std = sems("sub_std")
        sub_ready = sems("sub_ready")
        x_mid = sems("x_mid")
        ssq2 = sems("ssq2")
        var2 = sems("var2")
        std2 = sems("std2")
        h2_ready = sems("h2_ready")
        route_w_in = sems("route_w_in")
        pick_ready = sems("pick_ready")
        gexp_in = sems("gexp_in")
        gexp = sems("gexp")
        routed = sems("routed")
        scattered = sems("scattered")
        gates_in = sems("gates_in")
        hg_in = sems("hg_in")
        hg_ready = sems("hg_ready")
        hgt_full = sems("hgt_full")
        hgt_ready = sems("hgt_ready")
        gu_full = sems("gu_full")
        sg_ready = sems("sg_ready")
        hid_ready = sems("hid_ready")
        hidt_full = sems("hidt_full")
        hidt_ready = sems("hidt_ready")
        y_full = sems("y_full")
        y_ready = sems("y_ready")
        y_stored = sems("y_stored")
        y_free = sems("y_free")
        exp_used = sems("exp_used")
        y_back = [sems(f"y_back{i}") for i in range(2)]
        x_out = sems("x_out")
        fin_in = sem("fin_in")
        fssq = sem("fssq")
        fin_var = sem("fin_var")
        fin_std = sem("fin_std")
        fin_ready = sem("fin_ready")
        stored = sem("stored")
        pe_steps = sem("pe_steps")
        pool_steps = sem("pool_steps")
        dve_steps = sem("dve_steps")

        def full(eng, key):
            b, n = place[key]
            eng.wait_ge(bank_full[b], n + 1)

        def emptied(eng, key):
            b, n = place[key]
            eng.wait_ge(bank_read[b], n + 1)

        def ps(key):
            return bank[place[key][0]]

        def read_sem(key):
            return bank_read[place[key][0]]

        def last_product(l, item):
            if item[0] == "mod":
                return ("mod", item[1], item[2])
            if item[0] == "in":
                return [p for p in in_products(item[1]) if p[0] == item[2]][-1]
            return ("Y", item[1], query_tiles(item[1]) - 1, 1)

        fills = [0] * SLOTS
        slot_before, holder, load_waits = {}, [None] * SLOTS, {}
        pieces = 0
        for item, s in RING:
            if item[0] == "exp":
                slot_before[item] = [(s + j) % SLOTS for j in range(SLOTS)], list(fills)
                load_waits[item] = [holder[(s + j) % SLOTS] for j in range(SLOTS)]
                for j in range(SLOTS):
                    fills[j] += N_EXP // 2
                    holder[(s + j) % SLOTS] = ("exp", item[1], N_EXP - 2 + j // 3)
                continue
            load_waits[item] = holder[s]
            fills[s] += 2 if item[0] == "in" and item[2] == "E" else 1
            slot_before[item] = s, fills[s]
            if item[0] == "mod" and item[3] < 3:
                pieces += 1
                holder[s] = ("piece", pieces)
            else:
                holder[s] = ("product", last_product(None, item))

        def wait_free(eng, h):
            if h is None:
                return
            if h[0] == "piece":
                eng.wait_ge(mod_piece, h[1])
            elif h[0] == "product":
                full(eng, h[1])
            else:
                eng.wait_ge(exp_used[h[1]], h[2] + 1)

        def landed(eng, item):
            s, n = slot_before[item]
            eng.wait_ge(slot_in[s], 16 * n)
            return ring[:, s, :]

        def mix_half(kind, h):
            return h % 2

        def mix_chunk(kind, h):
            return {"na": 0, "gqa": 5}[kind] + h // 2

        def maxes(l, u, s):
            return sum(2 if k == "diff" else 1 for k, _, _ in head_units(l)[:u]) + s + 1

        R_M = 0
        R_GD, R_GE, R_C4, R_OG, R_PEN = 64, 80, 96, 112, 128
        R_E1, R_EQ, R_C16, R_O1, R_O2, R_X = 144, 208, 272, 336, 400, 464
        R_GM, R_GS, R_PG, R_CI, R_M1, R_I1, R_M2, R_I2, R_DM, R_E2, R_DEN, R_R = [528 + 4 * i for i in range(12)]
        R_TOT, R_CMP, R_NB, R_PA, R_PB = 576, 640, 752, 768, 784
        R_POS, R_RP, R_ROW, R_LOC = 800, 864, 928, 944

        def mod_loads(n, second):
            done_ = sum(1 if r == 1 else 2 for r in [0, 1, 2, 0, 1, 2][:n])
            return done_ + 1 + second

        N_CONST = 12

        block = ctx.enter_context(nc.Block())

        @block.sync
        def _(sp):
            def load_item(item):
                s, _ = slot_before[item]
                wait_free(sp, load_waits[item])
                if item[0] == "mod":
                    _, l, r, k = item
                    src = io["w_mod"][l, k * 256:(k + 1) * 256, r * 2048:(r + 1) * 2048]
                    sp.dma_start(ring[:, s, :].rearrange("p (a n) -> p a n", a=2),
                                 src.rearrange("(a p) n -> p a n", p=P)).then_inc(slot_in[s], 16)
                elif item[0] == "in":
                    _, l, g = item
                    width = sum(b - a for a, b in GROUPS[g])
                    dst = ring[:, s, 0:KD * width].rearrange("p (k n) -> p k n", k=KD)
                    at = 0
                    for a, b in GROUPS[g]:
                        sp.dma_start(dst[:, :, at:at + b - a],
                                     io["w_in"][l, :, a:b].rearrange("(k p) n -> p k n", p=P)).then_inc(slot_in[s], 16)
                        at += b - a
                else:
                    _, l, half = item
                    sp.dma_start(ring[:, s, :].rearrange("p (k n) -> p k n", k=4),
                                 io["w_out"][l, half * 512:(half + 1) * 512, :].rearrange("(k p) n -> p k n", p=P)
                                 ).then_inc(slot_in[s], 16)

            def load_expert(l, e, slots):
                for j, (w, k) in enumerate((("w_gate", 8), ("w_up", 8), ("w_down", 4))):
                    dst = ring[:, slots[j], :].rearrange("p (k n) -> p k n", k=k)
                    src = io[w][l, bass.ds(e, 1), :, :].rearrange("e (k p) n -> p (e k) n", p=P)
                    sp.dma_start(dst, src).then_inc(slot_in[slots[j]], 16)

            sp.dma_start(cond[:, :, 0], io["c"][0, :].rearrange("(k p) -> p k", p=P),
                         allow_slow_non_contiguous=True).then_inc(cond_in, 16)
            sp.dma_start(cond[:, :, 1], io["c_ctx"].rearrange("(k p) -> p k", p=P),
                         allow_slow_non_contiguous=True).then_inc(cond_in, 16)
            sp.dma_start(x_res[:, 0:XT, :], io["x"][0].rearrange("(t p) d -> p t d", p=P)).then_inc(x_in, 16)
            sp.dma_start(x_res[:, XT:, :], io["ctx"][0].rearrange("(t p) d -> p t d", p=P)).then_inc(x_in, 16)
            for item, _ in RING[:5]:
                load_item(item)
            sp.wait_ge(ga_in[1][0], 32)
            for item, _ in RING[5:]:
                if item[0] != "exp":
                    load_item(item)
                    if item == ("in", 0, "A"):
                        sp.wait_ge(zeroed, 1)
                        sp.dma_start(hbuf.rearrange("(p a) (b n) -> p (a b) n", p=P // 2, n=256),
                                     zeros[0:P // 2, :].unsqueeze(1).to_broadcast(
                                         [P // 2, (MAX_BLOCKS + HG_AHEAD) * 4, 256])).then_inc(hbuf_zero, 16)
                    continue
                l = item[1]
                slots, _ = slot_before[item]
                for j in range(SLOTS):
                    wait_free(sp, load_waits[item][j])
                    w, k = (("w_gate", 8), ("w_up", 8), ("w_down", 4))[j % 3]
                    sp.dma_start(ring[:, slots[j], :].rearrange("p (k n) -> p k n", k=k),
                                 io[w][l, j // 3].rearrange("(k p) n -> p k n", p=P)).then_inc(slot_in[slots[j]], 16)
                with sp.Fori(1, N_EXP // 2) as pair:
                    for u in range(2):
                        sp.wait_ge(exp_used[l], 2 * pair + (u - 1))
                        load_expert(l, 2 * pair + u, slots[3 * u:3 * u + 3])

        @block.tensor
        def _(pe):
            made = []

            def start(key):
                made.append(key)
                if before[key] is not None:
                    emptied(pe, before[key])
                return ps(key)

            def done(ins, key):
                ins.then_inc(bank_full[place[key][0]], 1)

            def mod(l, r, k):
                w = landed(pe, ("mod", l, r, k)).rearrange("p (a n) -> p a n", a=2)
                key = ("mod", l, r)
                if k == 0 and before[key] is not None:
                    emptied(pe, before[key])
                for a in range(2):
                    lhs = csil[:, 2 * k + a, :, :].rearrange("p o c -> p (o c)")
                    for j in range(4):
                        mm = pe.matmul(bank[7][32 * j:32 * j + 32, :], lhs, w[:, a, 512 * j:512 * j + 512],
                                       start=(k == 0 and a == 0), stop=(k == 3 and a == 1), tile_position=(0, 32 * j))
                if k == 3:
                    made.append(key)
                    done(mm, key)
                else:
                    mm.then_inc(mod_piece, 1)

            def mods(at):
                for m in mod_pieces_after(at):
                    mod(*m)

            def transposes(key, src, chunks, rows_in=P):
                dst = start(key)
                for c in range(chunks):
                    mm = pe.transpose(dst[:, c * P:c * P + rows_in], src[:, c * P:(c + 1) * P], ident[0:rows_in, 0:rows_in])
                done(mm, key)

            def in_product(key):
                kind, l, i = key
                nq = P * query_tiles(l)
                if kind == "F" or kind == "D" or kind == "C" or kind == "E":
                    w = landed(pe, ("in", l, kind))
                    n = sum(b - a for a, b in GROUPS[kind])
                    w = w[:, 0:KD * n].rearrange("p (k n) -> p k n", k=KD)
                    lo = 0
                    if i * P >= nq and kind in "FD":
                        lo = 384 if kind == "F" else 256
                    dst = start(key)
                    for k in range(KD):
                        mm = pe.matmul(dst[:, lo:n], h_t[:, k, i * P:(i + 1) * P], w[:, k, lo:n],
                                       start=(k == 0), stop=(k == KD - 1))
                    done(mm, key)
                elif kind in "AB":
                    w = landed(pe, ("in", l, kind))[:, 0:KD * 384].rearrange("p (k n) -> p k n", k=KD)
                    n = nq if kind == "A" else N_TOK
                    dst = start(key)
                    for k in range(KD):
                        mm = pe.matmul(dst[:, 0:n], w[:, k, i * P:(i + 1) * P], h_t[:, k, 0:n],
                                       start=(k == 0), stop=(k == KD - 1))
                    done(mm, key)
                elif kind == "Ft":
                    pe.wait_ge(rope_ready[l], i + 1)
                    lo = 0 if i * P < nq else 3
                    dst = start(key)
                    for c in range(lo, 4):
                        mm = pe.transpose(dst[:, c * P:(c + 1) * P], h_tok[:, i, c * P:(c + 1) * P], ident)
                    done(mm, key)
                else:
                    if i < XT:
                        pe.wait_ge(rope_ready[l], TILES + i + 1)
                    else:
                        pe.wait_ge(ctx_copied[l], i - XT + 1)
                    lo = 0 if i * P < nq else 2
                    dst = start(key)
                    for c in range(lo, 4):
                        mm = pe.transpose(dst[:, c * P:(c + 1) * P], h_tok[:, i, c * P:(c + 1) * P], ident)
                    done(mm, key)

            def scores(l, u):
                kind, h, x = head_units(l)[u]
                sets = 2 if kind == "diff" else 1
                n_k = N_TOK if x else CTX
                k0 = 0 if x else SEQ
                q0 = 0 if x else SEQ
                for s in range(sets):
                    if kind == "na":
                        qi, ki, qp, kp, w = Q_NA + h // 2, K_NA + h // 2, 64 * (h % 2), 64 * (h % 2), 64
                    elif kind == "gqa":
                        qi, ki, qp, kp, w = Q_GQ + h % 3, K_GQ, 64 * (h // 3), 64 * (h // 3), 64
                    else:
                        qi, ki, qp, kp, w = Q_DF + h // 2, K_DF + h // 2, 64 * (h % 2) + 32 * s, 64 * (h % 2) + 32 * s, 32
                    for q in range(2):
                        if x:
                            dst = start(("S", l, u, s, q))
                        elif q == 0:
                            dst = start(("S", l, u, s, 0))
                        if x and kind == "na" and h == 0:
                            pe.wait_ge(win_ready[l], 1)
                        o_ps = dst[:, 0:n_k] if x else dst[:, q * CTX:(q + 1) * CTX]
                        bias = x and kind == "na"
                        mm = pe.matmul(o_ps, qk[qp:qp + w, qi, q0 + q * P:q0 + (q + 1) * P],
                                       qk[kp:kp + w, ki, k0:k0 + n_k], start=True, stop=not bias,
                                       tile_position=(qp, 0))
                        if bias:
                            mm = pe.matmul(dst[:, 0:SEQ], cst[:, C_FLIP:C_FLIP + P], win[:, q, :, h, :], start=False, stop=True)
                        if x:
                            done(mm, ("S", l, u, s, q))
                        elif q == 1:
                            done(mm, ("S", l, u, s, 0))

            def turn_probs(l, u):
                kind, h, x = head_units(l)[u]
                pe.wait_ge(probs_ready[l], u + 1)
                p = prob[0] if kind == "diff" else prob[u % 2]
                if x:
                    for q in range(2):
                        transposes(("T", l, u, q), p[:, q, :], 4)
                else:
                    dst = start(("T", l, u, 0))
                    for kt in range(2):
                        for q in range(2):
                            mm = pe.transpose(dst[:, (2 * kt + q) * P:(2 * kt + q + 1) * P],
                                              p[:, q, kt * P:(kt + 1) * P], ident)
                    done(mm, ("T", l, u, 0))

            def weigh(l, u):
                kind, h, x = head_units(l)[u]
                for q in range(2 if x else 1):
                    emptied(pe, ("T", l, u, q))
                pt = prob_t[u % 2]
                kts = 4 if x else 2
                v0 = {"na": 64 * h, "diff": 384 + 64 * h, "gqa": 640 + 64 * (h // 3)}[kind]
                t0 = 0 if x else XT
                dst = start(("O", l, u))
                if kind == "diff":
                    for q in range(2):
                        for kt in range(kts):
                            mm = pe.matmul(dst[:, 64 * q:64 * q + 64], pt[:, kt, q * P:(q + 1) * P],
                                           v_tok[:, t0 + kt, v0:v0 + 64], start=(kt == 0), stop=(kt == kts - 1))
                else:
                    half = mix_half(kind, h)
                    for kt in range(kts):
                        mm = pe.matmul(dst[64 * half:64 * half + 64, 0:SEQ], v_tok[:, t0 + kt, v0:v0 + 64],
                                       pt[:, kt, :], start=(kt == 0), stop=(kt == kts - 1),
                                       tile_position=(0, 64 * half))
                done(mm, ("O", l, u))

            def out_product(l, t):
                for half in range(2):
                    key = ("Y", l, t, half)
                    dst = start(key)
                    for k in range(KD):
                        w = landed(pe, ("out", l, k // 4)).rearrange("p (k n) -> p k n", k=4)
                        mm = pe.matmul(dst[:, :], mixed[:, k, t * P:(t + 1) * P], w[:, k % 4, half * 512:half * 512 + 512],
                                       start=(k == 0), stop=(k == KD - 1))
                    done(mm, key)

            def experts(l):
                slots, filled = slot_before[("exp", l)]
                t_bank, gu, ht, yb = bank[0], (bank[1], bank[4]), (bank[2], bank[5]), bank[3]

                def turn_rows(g):
                    pe.wait_ge(hg_ready[l], g + 1)
                    pe.sem_inc(pe_steps, 1)
                    for k in range(KD):
                        mm = pe.transpose(t_bank[:, k * BLOCK:(k + 1) * BLOCK], hg[0:BLOCK, k * P:(k + 1) * P],
                                          ident[0:BLOCK, 0:BLOCK])
                    mm.then_inc(hgt_full[l], 1)

                def turn_hidden(g, half):
                    pe.wait_ge(hid_ready[l], 2 * g + (half + 1))
                    pe.sem_inc(pe_steps, 1)
                    for k in range(2):
                        c = 2 * half + k
                        mm = pe.transpose(ht[half][:, k * BLOCK:(k + 1) * BLOCK], hid[0:BLOCK, c * P:(c + 1) * P],
                                          ident[0:BLOCK, 0:BLOCK])
                    mm.then_inc(hidt_full[l], 1)

                for b in range(6):
                    last = [k for k in made if place[k][0] == b][-1]
                    emptied(pe, last)
                pe.wait_ge(routed[l], 1)
                turn_rows(0)
                with pe.Fori(0, N_EXP // 2) as pair:
                    for u in range(2):
                        n_blocks = pe.value_load(counts_i[0:1, bass.ds(2 * pair + u, 1)], min_val=1, max_val=8)
                        first = pe.value_load(counts_i[0:1, bass.ds(2 * pair + (N_EXP + u), 1)], min_val=0,
                                              max_val=MAX_BLOCKS)
                        wg, wu = [ring[:, slots[3 * u + j], :].rearrange("p (k n) -> p k n", k=8) for j in range(2)]
                        wd = ring[:, slots[3 * u + 2], :].rearrange("p (k n) -> p k n", k=4)
                        with pe.Fori(0, n_blocks) as i:
                            g = first + i
                            for j in range(2):
                                s = slots[3 * u + j]
                                pe.wait_ge(slot_in[s], 16 * pair + 16 * (filled[s] + 1))
                            pe.wait_ge(hgt_ready[l], g + 1)
                            for half in range(2):
                                cols = slice(256 * half, 256 * half + 256)
                                for k in range(KD):
                                    pe.matmul(gu[half][0:64, 0:256], hgt[:, k, :], wg[:, k, cols], start=(k == 0),
                                              stop=(k == KD - 1), tile_position=(0, 0))
                                    mm = pe.matmul(gu[half][64:128, 0:256], hgt[:, k, :], wu[:, k, cols],
                                                   start=(k == 0), stop=(k == KD - 1), tile_position=(0, 64))
                                mm.then_inc(gu_full[l], 1)
                            turn_hidden(g, 0)
                            turn_rows(g + 1)
                            turn_hidden(g, 1)
                            s = slots[3 * u + 2]
                            pe.wait_ge(slot_in[s], 16 * pair + 16 * (filled[s] + 1))
                            for half in range(2):
                                pe.wait_ge(hidt_ready[l], 2 * g + (half + 1))
                                for k in range(2 * half, 2 * half + 2):
                                    pe.matmul(yb[0:64, :], hidt[:, k, :], wd[:, k, 0:512], start=(k == 0),
                                              stop=(k == 3), tile_position=(0, 0))
                                    mm = pe.matmul(yb[64:128, :], hidt[:, k, :], wd[:, k, 512:1024], start=(k == 0),
                                                   stop=(k == 3), tile_position=(0, 64))
                            mm.then_inc(y_full[l], 1)
                        pe.wait_ge(y_full[l], first + n_blocks)
                        pe.sem_inc(exp_used[l], 1)
                n_all = pe.value_load(counts_i[0:1, 2 * N_EXP:2 * N_EXP + 1], min_val=1, max_val=MAX_BLOCKS)
                pe.wait_ge(y_ready[l], n_all)
                pe.wait_ge(hgt_ready[l], n_all + 1)

            pe.wait_ge(csil_ready, 1)
            for k in range(4):
                mod(0, 0, k)
            pe.wait_ge(consts_in, 16 * N_CONST)
            for l in range(LAYERS):
                for t in range(TILES):
                    pe.wait_ge(h_ready[l], t + 1)
                    for half in range(2):
                        transposes(("tr1", l, t, half), h_tok[:, t, half * 512:(half + 1) * 512], 4)
                for t in range(TILES):
                    for half in range(2):
                        emptied(pe, ("tr1", l, t, half))
                for n, key in enumerate(in_products(l)):
                    in_product(key)
                    if l == 0:
                        mods(("in", n))
                for key in in_products(l):
                    if key[0] in ("A", "B", "C", "E", "Ft", "Dt"):
                        emptied(pe, key)
                units = head_units(l)
                scores(l, 0)
                for u in range(len(units) + 1):
                    if u + 1 < len(units):
                        scores(l, u + 1)
                    if u < len(units):
                        turn_probs(l, u)
                    if u >= 1:
                        weigh(l, u - 1)
                    if l == 0:
                        mods(("unit", u))
                pe.wait_ge(sub_ready[l], 1)
                for t in range(query_tiles(l)):
                    transposes(("OBt", l, t), ob[:, t, :], 2)
                emptied(pe, ("O", l, len(units) - 1))
                for t in range(query_tiles(l)):
                    emptied(pe, ("OBt", l, t))
                for t in range(query_tiles(l) + 1):
                    if t < query_tiles(l):
                        out_product(l, t)
                    if t >= 1:
                        pe.wait_ge(h2_ready[l], t)
                        for half in range(2):
                            transposes(("tr2", l, t - 1, half), h_tok[:, t - 1, half * 512:(half + 1) * 512], 4)
                nt = query_tiles(l)
                for t in range(nt):
                    for half in range(2):
                        emptied(pe, ("tr2", l, t, half))
                pe.wait_ge(route_w_in[l], 32)
                dst = start(("R", l))
                for k in range(KD):
                    mm = pe.matmul(dst[0:20, 0:nt * P], w_route[:, k, :], h_t[:, k, 0:nt * P], start=(k == 0),
                                   stop=(k == KD - 1))
                done(mm, ("R", l))
                emptied(pe, ("R", l))
                dst = start(("Rt", l))
                for t in range(nt):
                    mm = pe.transpose(dst[:, 20 * t:20 * t + 20], lgt_t[0:20, t * P:(t + 1) * P], ident[0:20, 0:20])
                done(mm, ("Rt", l))
                pe.wait_ge(pick_ready[l], 1)
                dst = start(("cum", l))
                picked = rt[:, 0:16 * nt]
                pe.matmul(dst[:, 0:16 * nt], cst[:, C_TRI:C_TRI + P], picked, start=True, stop=True)
                mm = pe.matmul(dst[:, 64:64 + 16 * nt], cst[:, C_ONE:C_ONE + 1].to_broadcast([P, P]), picked, start=True, stop=True)
                done(mm, ("cum", l))
                experts(l)
            assert made == ORDER, [(a, b) for a, b in zip(made, ORDER) if a != b][:4]

        @block.scalar
        def _(act):
            def release(ins, key):
                ins.then_inc(read_sem(key), 1)

            def norm_stats(ready, base, got, sq_sem, var_sem, std_sem, t, scratch):
                act.wait_ge(ready, got)
                act.activation(scratch, x_res[:, t, :], ACT.Square, accum_out=stat[:, base + t:base + t + 1]
                               ).then_inc(sq_sem, 1)
                act.wait_ge(var_sem, t + 1)
                act.activation(stat[:, base + 8 + t:base + 9 + t], stat[:, base + 4 + t:base + 5 + t], ACT.Sqrt
                               ).then_inc(std_sem, 1)

            act.wait_ge(cond_in, 32)
            act.activation(csil[:, :, :, :], cond[:, :, :].unsqueeze(2).to_broadcast([P, KD, 16, 2]), ACT.Silu).then_inc(csil_ready, 1)
            act.wait_ge(lam_dots, 1)
            act.activation(stat[:, 72:76], stat[:, 68:72], ACT.Exp).then_inc(lam_exp, 1)
            for l in range(LAYERS):
                nt = query_tiles(l)
                nq = nt * P
                for t in range(TILES):
                    if l == 0:
                        norm_stats(x_in, 0, 32, ssq[l], var[l], std[l], t, h_tok[:, t, :])
                    else:
                        norm_stats(x_out[0], 0, t + 1, ssq[l], var[l], std[l], t, h_tok[:, t, :])
                for t in range(TILES):
                    for half in range(2):
                        key = ("tr1", l, t, half)
                        full(act, key)
                        release(act.copy(h_t[:, 4 * half:4 * half + 4, t * P:(t + 1) * P],
                                         ps(key)[:, :].rearrange("p (k t) -> p k t", k=4)), key)
                for t in range(TILES):
                    key = ("F", l, t)
                    lo = 0 if t < nt else 384
                    full(act, key)
                    act.activation(h_tok[:, t, 512 + lo:1024], ps(key)[:, lo:512], ACT.Square).then_inc(fsq[l], 1)
                    act.wait_ge(fvar[l], t + 1)
                    act.activation(fstat[:, 1, lo // 64:8], fstat[:, 0, lo // 64:8], ACT.Sqrt).then_inc(fstd[l], 1)
                for kind in ("Ft", "A", "Dt"):
                    if kind == "A":
                        for t in range(XT, TILES):
                            key = ("D", l, t)
                            lo = 0 if t < nt else 256
                            full(act, ("Ft", l, t))
                            full(act, key)
                            act.copy(h_tok[:, t, lo:512], ps(key)[:, lo:512]).then_inc(ctx_copied[l], 1)
                            act.wait_ge(ctx_copied[l], t - XT + 1)
                            act.sem_inc(read_sem(key), 1)
                        for m in range(3):
                            key = ("A", l, m)
                            full(act, key)
                            release(act.mul(qk[:, Q_NA + m, 0:nq], ps(key)[:, 0:nq], 64 ** -0.5), key)
                        continue
                    n_q, q0, k0, scale = (3, Q_GQ, K_GQ, 64 ** -0.5) if kind == "Ft" else (2, Q_DF, K_DF, 32 ** -0.5)
                    for t in range(TILES):
                        key = (kind, l, t)
                        full(act, key)
                        v = ps(key)[:, :].rearrange("p (c t) -> p c t", c=4)
                        if t < nt:
                            act.mul(qk[:, q0:q0 + n_q, t * P:(t + 1) * P], v[:, 0:n_q, :], scale)
                        release(act.copy(qk[:, k0:k0 + 4 - n_q, t * P:(t + 1) * P], v[:, n_q:4, :]), key)
                units = head_units(l)

                def exps(u):
                    kind, h, x = units[u]
                    if u >= 1 and (kind == "diff" or units[u - 1][0] == "diff"):
                        full(act, ("T", l, u - 1, 1 if units[u - 1][2] else 0))
                    if u >= 2:
                        full(act, ("T", l, u - 2, 1 if units[u - 2][2] else 0))
                    if u == 0:
                        full(act, ("Dt", l, TILES - 1))
                    for s in range(2 if kind == "diff" else 1):
                        act.wait_ge(max_ready[l], maxes(l, u, s))
                        buf = s if kind == "diff" else u % 2
                        for q in range(2):
                            n = 2 * buf + q
                            b = ps(("S", l, u, s, q if x else 0))
                            src = b[:, 0:N_TOK] if x else b[:, q * CTX:(q + 1) * CTX]
                            act.activation(prob[buf][:, q, 0:N_TOK if x else CTX], src, ACT.Exp,
                                           bias=stat[:, 48 + n:49 + n], accum_out=stat[:, 52 + n:53 + n]
                                           ).then_inc(exp_ready[l], 1)

                def out_t(u):
                    kind, h, x = units[u]
                    key = ("O", l, u)
                    if kind == "diff":
                        return
                    full(act, key)
                    half = mix_half(kind, h)
                    q0 = 0 if x else SEQ
                    release(act.copy(mixed[64 * half:64 * half + 64, mix_chunk(kind, h), q0:q0 + SEQ],
                                     ps(key)[64 * half:64 * half + 64, 0:SEQ]), key)

                exps(0)
                for u in range(len(units) + 1):
                    if u + 1 < len(units):
                        exps(u + 1)
                    if u < len(units):
                        if units[u][2]:
                            key = ("T", l, u, 1)
                            if u >= 2:
                                full(act, ("O", l, u - 2))
                            full(act, key)
                            release(act.copy(prob_t[u % 2][:, :, P:2 * P],
                                             ps(key)[:, :].rearrange("p (k q) -> p k q", k=4)), key)
                    if u >= 1:
                        out_t(u - 1)
                act.wait_ge(sub_var[l], 1)
                act.activation(stat[:, 16:16 + 4 * nt], stat[:, 0:4 * nt], ACT.Sqrt).then_inc(sub_std[l], 1)
                for t in range(nt):
                    key = ("OBt", l, t)
                    full(act, key)
                    release(act.copy(mixed[:, 3:5, t * P:(t + 1) * P],
                                     ps(key)[:, 0:256].rearrange("p (k t) -> p k t", k=2)), key)
                for t in range(nt + 1):
                    if t < nt:
                        norm_stats(x_mid[l], 0, t + 1, ssq2[l], var2[l], std2[l], t, h_tok[:, t, :])
                    if t >= 1:
                        for half in range(2):
                            key = ("tr2", l, t - 1, half)
                            full(act, key)
                            release(act.copy(h_t[:, 4 * half:4 * half + 4, (t - 1) * P:t * P],
                                             ps(key)[:, :].rearrange("p (k t) -> p k t", k=4)), key)
                full(act, ("R", l))
                release(act.copy(lgt_t[0:20, 0:nt * P], ps(("R", l))[0:20, 0:nt * P]), ("R", l))
                act.wait_ge(gexp_in[l], 1)
                act.activation(rt[:, R_GE:R_GE + 4 * nt], rt[:, R_GD:R_GD + 4 * nt], ACT.Exp).then_inc(gexp[l], 1)
                act.wait_ge(gexp_in[l], 2)
                act.activation(rt[:, R_E2:R_E2 + nt], rt[:, R_DM:R_DM + nt], ACT.Exp).then_inc(gexp[l], 1)
                act.wait_ge(routed[l], 1)
                n_all = act.value_load(counts_i[0:1, 2 * N_EXP:2 * N_EXP + 1], min_val=1, max_val=MAX_BLOCKS)

                act.wait_ge(hgt_full[l], 1)
                act.copy(hgt[:, :, :], bank[0][:, :].rearrange("p (k r) -> p k r", k=KD)).then_inc(hgt_ready[l], 1)
                with act.Fori(0, n_all) as g:
                    for half in range(2):
                        act.wait_ge(gu_full[l], 2 * g + (half + 1))
                        act.activation(sg[0:BLOCK, 256 * half:256 * half + 256], bank[(1, 4)[half]][0:BLOCK, 0:256],
                                       ACT.Silu).then_inc(sg_ready[l], 1)
                    act.wait_ge(hgt_full[l], g + 2)
                    act.copy(hgt[:, :, :], bank[0][:, :].rearrange("p (k r) -> p k r", k=KD)).then_inc(hgt_ready[l], 1)
            for t in range(XT):
                norm_stats(x_out[LAYERS - 1], 32, t + 1, fssq, fin_var, fin_std, t, h_tok[:, t, :])

        @block.vector
        def _(dve):
            chain = [0]

            def link(ins):
                chain[0] += 1
                ins.then_inc(dve_order, 1)
                dve.wait_ge(dve_order, chain[0])

            def release(ins, key):
                ins.then_inc(read_sem(key), 1)

            def norm(l, base, t, sq_sem, var_sem, std_sem, a_row, s_row, dst):
                dve.wait_ge(sq_sem, t + 1)
                dve.tensor_scalar(stat[:, base + 4 + t:base + 5 + t], stat[:, base + t:base + t + 1], 1.0 / D, EPS,
                                  ALU.mult, ALU.add).then_inc(var_sem, 1)
                dve.wait_ge(std_sem, t + 1)
                link(dve.reciprocal(stat[:, base + 12 + t:base + 13 + t], stat[:, base + 8 + t:base + 9 + t]))
                ins = dve.scalar_tensor_tensor(dst, x_res[:, t, :], stat[:, base + 12 + t:base + 13 + t], a_row,
                                               ALU.mult, ALU.mult)
                if s_row is not None:
                    link(ins)
                    ins = dve.tensor_tensor(dst, dst, s_row, ALU.add)
                return ins

            def mod_rows(l, r, n):
                key = ("mod", l, r)
                full(dve, key)
                dve.wait_ge(mod_b_in, 16 * mod_loads(n, 0))
                if n >= 1:
                    dve.wait_ge(mod_stored, 32 * n)
                dve.tensor_tensor(mod_row, bank[7][:, :], mod_add, ALU.add).then_inc(mod_sum, 1)
                dve.wait_ge(mod_sum, n + 1)
                dve.sem_inc(read_sem(key), 1)
                if r != 1:
                    rows_p = slice(64, 128) if r == 0 else slice(0, 64)
                    dve.wait_ge(mod_b_in, 16 * mod_loads(n, 1))
                    dve.scalar_tensor_tensor(mod_row[rows_p, :], mod_row[rows_p, :], 1.0, mod_add[rows_p, :],
                                             ALU.add, ALU.mult).then_inc(mod_done, 1)
                else:
                    dve.sem_inc(mod_done, 1)

            rounds = [(0, 0), (0, 1), (0, 2), (1, 0), (1, 1), (1, 2)]

            def mods(at):
                for l, r, k in mod_pieces_after(at):
                    if k == 3:
                        mod_rows(l, r, rounds.index((l, r)))

            def rope(dst, src, tmp, groups, dim, cc, ss):
                v = src.rearrange("p (g d) -> p g d", d=dim)
                o_ = dst.rearrange("p (g d) -> p g d", d=dim)
                t_ = tmp.rearrange("p (g d) -> p g d", d=dim)
                h = dim // 2
                cb = cc.unsqueeze(1).to_broadcast([P, groups, dim])
                s1 = ss[:, 0:h].unsqueeze(1).to_broadcast([P, groups, h])
                s2 = ss[:, h:dim].unsqueeze(1).to_broadcast([P, groups, h])
                dve.tensor_tensor(o_, v, cb, ALU.mult)
                dve.tensor_tensor(t_[:, :, 0:h], v[:, :, h:dim], s1, ALU.mult)
                link(dve.tensor_tensor(t_[:, :, h:dim], v[:, :, 0:h], s2, ALU.mult))

            dve.memset(zeros[:, :], 0.0).then_inc(zeroed, 1)
            dve.wait_ge(consts_in, 16 * N_CONST)
            lq = h_tok[:, 0, 0:256].rearrange("p (v l d) -> p v l d", v=4, l=LAYERS)
            pr = h_tok[:, 0, 256:384].rearrange("p (v l d) -> p v l d", v=2, l=LAYERS)
            for i in range(2):
                ins = dve.tensor_tensor(pr[:, i], lq[:, 2 * i], lq[:, 2 * i + 1], ALU.mult)
            link(ins)
            dve.tensor_reduce(stat[:, 68:72], h_tok[:, 0, 256:384].rearrange("p (a d) -> p a d", d=32), AX.X,
                              ALU.add).then_inc(lam_dots, 1)
            dve.wait_ge(lam_exp, 1)
            for l in range(LAYERS):
                lam_init = 0.8 - 0.6 * math.exp(-0.3 * l)
                link(dve.tensor_tensor(neglam[:, l:l + 1], stat[:, 74 + l:75 + l], stat[:, 72 + l:73 + l], ALU.subtract))
                link(dve.tensor_scalar(neglam[:, l:l + 1], neglam[:, l:l + 1], -lam_init, None, ALU.add))
                link(dve.tensor_scalar(subg[:, l, :], subg[:, l, :], 1.0 - lam_init, None, ALU.mult))
            mod_rows(0, 0, 0)

            for l in range(LAYERS):
                nt = query_tiles(l)
                for t in range(TILES):
                    a_row, s_row = (2, 3) if t < XT else (0, 1)
                    if t == 0:
                        dve.wait_ge(ga_in[0][l], 32)
                    if t == XT:
                        dve.wait_ge(ga_in[1][l], 32)
                    norm(l, 0, t, ssq[l], var[l], std[l], rows[:, a_row, :], rows[:, s_row, :],
                         h_tok[:, t, :]).then_inc(h_ready[l], 1)
                n_in = [0]

                def after_in():
                    if l == 0:
                        mods(("in", n_in[0]))
                    n_in[0] += 1

                for t in range(TILES):
                    key = ("F", l, t)
                    q_heads = 6 if t < nt else 0
                    g0 = 6 - q_heads
                    lo = 64 * g0
                    b = ps(key)
                    hi_ = h_tok[:, t, 512 + lo:1024]
                    lo_ = h_tok[:, t, lo:512]
                    dve.wait_ge(fsq[l], t + 1)
                    link(dve.tensor_reduce(fstat[:, 2, g0:8], hi_.rearrange("p (g d) -> p g d", d=64), AX.X, ALU.add))
                    dve.tensor_scalar(fstat[:, 0, g0:8], fstat[:, 2, g0:8], 1.0 / 64, EPS, ALU.mult,
                                      ALU.add).then_inc(fvar[l], 1)
                    dve.wait_ge(fstd[l], t + 1)
                    link(dve.reciprocal(fstat[:, 2, g0:8], fstat[:, 1, g0:8]))
                    link(dve.tensor_tensor(hi_.rearrange("p (g d) -> p g d", d=64),
                                           b[:, lo:512].rearrange("p (g d) -> p g d", d=64),
                                           fstat[:, 2, g0:8].unsqueeze(2).to_broadcast([P, 8 - g0, 64]), ALU.mult))
                    dst = b if t < XT else h_tok[:, t, :]
                    if q_heads:
                        dve.tensor_tensor(dst[:, 0:384].rearrange("p (m h d) -> p h m d", m=3, h=2),
                                          h_tok[:, t, 512:896].rearrange("p (h m d) -> p h m d", m=3, h=2),
                                          gains[:, l, 0, :].unsqueeze(1).unsqueeze(1).to_broadcast([P, 2, 3, 64]),
                                          ALU.mult)
                    ins = dve.tensor_tensor(dst[:, 384:512].rearrange("p (g d) -> p g d", d=64),
                                            h_tok[:, t, 896:1024].rearrange("p (g d) -> p g d", d=64),
                                            gains[:, l, 1, :].unsqueeze(1).to_broadcast([P, 2, 64]), ALU.mult)
                    if t < XT:
                        link(ins)
                        rope(lo_, b[:, 0:512], hi_, 8, 64, cst[:, C_C32 + 64 * t:C_C32 + 64 * t + 64],
                             cst[:, C_S32 + 64 * t:C_S32 + 64 * t + 64])
                        dve.tensor_tensor(lo_, lo_, hi_, ALU.add).then_inc(rope_ready[l], 1)
                    else:
                        ins.then_inc(rope_ready[l], 1)
                    dve.wait_ge(rope_ready[l], t + 1)
                    dve.sem_inc(read_sem(key), 1)
                    after_in()
                for t in range(TILES):
                    if t < XT:
                        key = ("D", l, t)
                        full(dve, ("Ft", l, t))
                        full(dve, key)
                        lo_, hi_ = h_tok[:, t, 0:512], h_tok[:, t, 512:1024]
                        rope(lo_, ps(key)[:, 0:512], hi_, 16, 32, cst[:, C_C16 + 32 * t:C_C16 + 32 * t + 32],
                             cst[:, C_S16 + 32 * t:C_S16 + 32 * t + 32])
                        dve.tensor_tensor(lo_, lo_, hi_, ALU.add).then_inc(rope_ready[l], 1)
                        dve.wait_ge(rope_ready[l], TILES + t + 1)
                        dve.sem_inc(read_sem(key), 1)
                    after_in()
                dve.wait_ge(ga_in[2][l], 64)
                dve.tensor_tensor(rows[:, 0:3, :].rearrange("p a b -> p (a b)").rearrange("p (g c) -> p g c", c=64),
                                  rows[:, 0:3, :].rearrange("p a b -> p (a b)").rearrange("p (g c) -> p g c", c=64),
                                  cst[:, C_MASK:C_MASK + 64].unsqueeze(1).to_broadcast([P, 48, 64]),
                                  ALU.add).then_inc(win_ready[l], 1)
                for p in in_products(l)[2 * TILES:]:
                    if p[0] == "B":
                        full(dve, p)
                        release(dve.tensor_copy(qk[:, K_NA + p[2], :], ps(p)[:, :]), p)
                    elif p[0] == "C":
                        full(dve, p)
                        release(dve.tensor_copy(v_tok[:, p[2], 0:384], ps(p)[:, 0:384]), p)
                    elif p[0] == "E":
                        full(dve, p)
                        release(dve.tensor_copy(v_tok[:, p[2], 384:768], ps(p)[:, 0:384]), p)
                    after_in()
                units = head_units(l)

                def maxima(u):
                    kind, h, x = units[u]
                    for s in range(2 if kind == "diff" else 1):
                        buf = s if kind == "diff" else u % 2
                        for q in range(2):
                            k_ = ("S", l, u, s, q if x else 0)
                            full(dve, k_)
                            src = ps(k_)[:, 0:N_TOK] if x else ps(k_)[:, q * CTX:(q + 1) * CTX]
                            ins = dve.tensor_reduce(stat[:, 48 + 2 * buf + q:49 + 2 * buf + q], src, AX.X, ALU.max,
                                                    negate=True)
                        ins.then_inc(max_ready[l], 1)

                def exp_count(u):
                    return sum(4 if k == "diff" else 2 for k, _, _ in units[:u + 1])

                def normalise(u):
                    kind, h, x = units[u]
                    n_k = N_TOK if x else CTX
                    dve.wait_ge(exp_ready[l], exp_count(u))
                    for s in range(2 if kind == "diff" else 1):
                        for q in range(2 if x else 1):
                            dve.sem_inc(read_sem(("S", l, u, s, q)), 1)
                    if kind == "diff":
                        link(dve.reciprocal(stat[:, 56:60], stat[:, 52:56]))
                        link(dve.tensor_scalar(stat[:, 58:60], stat[:, 58:60], neglam[:, l:l + 1], None, ALU.mult))
                        for q in range(2):
                            ins = dve.tensor_scalar(prob[1][:, q, 0:n_k], prob[1][:, q, 0:n_k],
                                                    stat[:, 58 + q:59 + q], None, ALU.mult)
                        link(ins)
                        for q in range(2):
                            ins = dve.scalar_tensor_tensor(prob[0][:, q, 0:n_k], prob[0][:, q, 0:n_k],
                                                           stat[:, 56 + q:57 + q], prob[1][:, q, 0:n_k],
                                                           ALU.mult, ALU.add)
                    else:
                        n = 2 * (u % 2)
                        link(dve.reciprocal(stat[:, 56 + n:58 + n], stat[:, 52 + n:54 + n]))
                        for q in range(2):
                            ins = dve.tensor_scalar(prob[u % 2][:, q, 0:n_k], prob[u % 2][:, q, 0:n_k],
                                                    stat[:, 56 + n + q:57 + n + q], None, ALU.mult)
                    ins.then_inc(probs_ready[l], 1)

                def turned(u):
                    kind, h, x = units[u]
                    key = ("T", l, u, 0)
                    if u >= 2:
                        full(dve, ("O", l, u - 2))
                    full(dve, key)
                    if x:
                        release(dve.tensor_copy(prob_t[u % 2][:, :, 0:P],
                                                ps(key)[:, :].rearrange("p (k q) -> p k q", k=4)), key)
                    else:
                        release(dve.tensor_copy(prob_t[u % 2][:, 0:2, :],
                                                ps(key)[:, :].rearrange("p (k q) -> p k q", k=2)), key)

                def out_rows(u):
                    kind, h, x = units[u]
                    if kind == "diff":
                        key = ("O", l, u)
                        full(dve, key)
                        t0 = 0 if x else XT
                        release(dve.tensor_copy(ob[:, t0:t0 + 2, 64 * h:64 * h + 64],
                                                ps(key)[:, 0:128].rearrange("p (q d) -> p q d", q=2)), key)

                maxima(0)
                for u in range(len(units) + 1):
                    if u < len(units):
                        normalise(u)
                    if u + 1 < len(units):
                        maxima(u + 1)
                    if u < len(units):
                        turned(u)
                    if u >= 1:
                        out_rows(u - 1)
                    if l == 0:
                        mods(("unit", u))
                sq = ob_sq[:, 0:256 * nt]
                obv = big[:, 0:256 * nt]
                link(dve.tensor_tensor(sq, obv, obv, ALU.mult))
                link(dve.tensor_reduce(stat[:, 32:32 + 4 * nt], sq.rearrange("p (g d) -> p g d", d=64), AX.X, ALU.add))
                dve.tensor_scalar(stat[:, 0:4 * nt], stat[:, 32:32 + 4 * nt], 1.0 / 64, EPS, ALU.mult,
                                  ALU.add).then_inc(sub_var[l], 1)
                dve.wait_ge(sub_std[l], 1)
                link(dve.reciprocal(stat[:, 32:32 + 4 * nt], stat[:, 16:16 + 4 * nt]))
                og = obv.rearrange("p (g d) -> p g d", d=64)
                link(dve.tensor_tensor(og, og, stat[:, 32:32 + 4 * nt].unsqueeze(2).to_broadcast([P, 4 * nt, 64]),
                                       ALU.mult))
                dve.tensor_tensor(og, og, subg[:, l, :].unsqueeze(1).to_broadcast([P, 4 * nt, 64]),
                                  ALU.mult).then_inc(sub_ready[l], 1)
                dve.wait_ge(gates_in[l], 16 * (nt // 2))
                def residual(t):
                    for half in range(2):
                        key = ("Y", l, t, half)
                        cols = slice(512 * half, 512 * half + 512)
                        full(dve, key)
                        ins = dve.tensor_tensor(h_tok[:, t, cols], ps(key)[:, :], rows[:, 0 if t < XT else 1, cols],
                                                ALU.mult)
                        release(ins, key)
                        emptied(dve, key)
                        ins = dve.tensor_tensor(x_res[:, t, cols], x_res[:, t, cols], h_tok[:, t, cols], ALU.add)
                    ins.then_inc(x_mid[l], 1)

                for t in range(nt):
                    residual(t)
                    if t == 0:
                        dve.wait_ge(ga_in[0][l], 64)
                    if t == XT:
                        dve.wait_ge(ga_in[1][l], 64)
                    a_row, s_row = (rows[:, 2, :], rows[:, 3, :]) if t < XT else (next_rows[:, 0, :], next_rows[:, 1, :])
                    norm(l, 0, t, ssq2[l], var2[l], std2[l], a_row, s_row, h_tok[:, t, :]).then_inc(h2_ready[l], 1)

                def r_(c, n):
                    return rt[:, c:c + n]

                def by_tile(c, n):
                    return rt[:, c:c + n * nt].rearrange("p (t n) -> p t n", t=nt)

                def spread(c, n):
                    return rt[:, c:c + nt].unsqueeze(2).to_broadcast([P, nt, n])

                lgv = lg[:, 0:20 * nt].rearrange("p (t n) -> p t n", t=nt)
                key = ("Rt", l)
                full(dve, key)
                dve.tensor_tensor(lgv, ps(key)[:, 0:20 * nt].rearrange("p (t n) -> p t n", t=nt),
                                  rbias[:, l, :].unsqueeze(1).to_broadcast([P, nt, 20]), ALU.add
                                  ).then_inc(read_sem(key), 1)
                emptied(dve, key)
                link(dve.tensor_reduce(r_(R_GM, nt), lgv[:, :, 0:4], AX.X, ALU.max))
                dve.tensor_tensor(by_tile(R_GD, 4), lgv[:, :, 0:4], spread(R_GM, 4), ALU.subtract).then_inc(gexp_in[l], 1)
                dve.wait_ge(gexp_in[l], 1)
                link(dve.tensor_scalar(r_(R_C4, 4 * nt), r_(R_GD, 4 * nt), 0.0, None, ALU.is_ge))
                ig = cst[:, C_IG:C_IG + 4].unsqueeze(1).to_broadcast([P, nt, 4])
                ie = cst[:, C_IE:C_IE + 16].unsqueeze(1).to_broadcast([P, nt, 16])
                link(dve.tensor_tensor(by_tile(R_C4, 4), by_tile(R_C4, 4), ig, ALU.mult))
                link(dve.tensor_reduce(r_(R_CI, nt), by_tile(R_C4, 4), AX.X, ALU.min))
                link(dve.tensor_tensor(by_tile(R_OG, 4), ig, spread(R_CI, 4), ALU.is_equal))
                link(dve.tensor_scalar(r_(R_PEN, 4 * nt), r_(R_OG, 4 * nt), -1.0, BIG, ALU.add, ALU.mult))
                for t in range(nt):
                    ins = dve.tensor_tensor(r_(R_E1 + 16 * t, 16).rearrange("p (g e) -> p g e", g=4),
                                            lgv[:, t, 4:20].rearrange("p (g e) -> p g e", g=4),
                                            r_(R_PEN + 4 * t, 4).unsqueeze(2).to_broadcast([P, 4, 4]), ALU.add)
                link(ins)

                def first_largest(src, m, idx, hot):
                    link(dve.tensor_reduce(r_(m, nt), by_tile(src, 16), AX.X, ALU.max))
                    link(dve.tensor_tensor(by_tile(R_EQ, 16), by_tile(src, 16), spread(m, 16), ALU.is_equal))
                    link(dve.tensor_tensor(by_tile(R_EQ, 16), by_tile(R_EQ, 16), ie, ALU.mult))
                    link(dve.tensor_reduce(r_(idx, nt), by_tile(R_EQ, 16), AX.X, ALU.min))
                    link(dve.tensor_tensor(by_tile(hot, 16), ie, spread(idx, 16), ALU.is_equal))

                first_largest(R_E1, R_M1, R_I1, R_O1)
                link(dve.scalar_tensor_tensor(r_(R_X, 16 * nt), r_(R_O1, 16 * nt), -BIG, r_(R_E1, 16 * nt), ALU.mult,
                                              ALU.add))
                first_largest(R_X, R_M2, R_I2, R_O2)
                dve.tensor_tensor(r_(R_M, 16 * nt), r_(R_O1, 16 * nt), r_(R_O2, 16 * nt), ALU.add
                                  ).then_inc(pick_ready[l], 1)
                dve.tensor_tensor(r_(R_DM, nt), r_(R_M2, nt), r_(R_M1, nt), ALU.subtract).then_inc(gexp_in[l], 1)
                dve.wait_ge(gexp[l], 1)
                link(dve.tensor_reduce(r_(R_GS, nt), by_tile(R_GE, 4), AX.X, ALU.add))
                link(dve.reciprocal(r_(R_PG, nt), r_(R_GS, nt)))
                dve.wait_ge(gexp[l], 2)
                link(dve.tensor_scalar(r_(R_DEN, nt), r_(R_E2, nt), 1.0, None, ALU.add))
                link(dve.reciprocal(r_(R_R, nt), r_(R_DEN, nt)))
                link(dve.tensor_tensor(wsel[:, 0, 0:nt], r_(R_R, nt), r_(R_PG, nt), ALU.mult))
                link(dve.tensor_tensor(wsel[:, 1, 0:nt], wsel[:, 0, 0:nt], r_(R_E2, nt), ALU.mult))
                key = ("cum", l)
                full(dve, key)
                dve.tensor_copy(r_(R_LOC, 16 * nt), ps(key)[:, 0:16 * nt])
                dve.tensor_copy(r_(R_TOT, 16 * nt), ps(key)[:, 64:64 + 16 * nt]).then_inc(read_sem(key), 1)
                emptied(dve, key)
                dve.tensor_copy(r_(R_POS, 16), r_(R_LOC, 16))
                for t in range(1, nt):
                    dve.tensor_tensor(r_(R_POS + 16 * t, 16), r_(R_LOC + 16 * t, 16), r_(R_TOT + 16 * (t - 1), 16),
                                      ALU.add)
                    link(dve.tensor_tensor(r_(R_TOT + 16 * t, 16), r_(R_TOT + 16 * t, 16), r_(R_TOT + 16 * (t - 1), 16),
                                           ALU.add))
                n_thr = nt * P // BLOCK - 1
                cmp = r_(R_CMP, 16 * n_thr).rearrange("p (e j) -> p e j", e=16)
                link(dve.tensor_tensor(cmp, r_(R_TOT + 16 * (nt - 1), 16).unsqueeze(2).to_broadcast([P, 16, n_thr]),
                                       cst[:, C_THR:C_THR + n_thr].unsqueeze(1).to_broadcast([P, 16, n_thr]),
                                       ALU.is_gt))
                link(dve.tensor_reduce(r_(R_NB, 16), cmp, AX.X, ALU.add))
                link(dve.tensor_scalar(r_(R_NB, 16), r_(R_NB, 16), 1.0, None, ALU.add))
                link(dve.tensor_copy(r_(R_PA, 16), r_(R_NB, 16)))
                a, b = R_PA, R_PB
                for d in (1, 2, 4, 8):
                    dve.tensor_copy(r_(b, d), r_(a, d))
                    link(dve.tensor_tensor(r_(b + d, 16 - d), r_(a + d, 16 - d), r_(a, 16 - d), ALU.add))
                    a, b = b, a
                link(dve.tensor_tensor(r_(b, 16), r_(a, 16), r_(R_NB, 16), ALU.subtract))
                dve.tensor_copy(counts_i[:, 0:16], r_(R_NB, 16))
                dve.tensor_copy(counts_i[:, 16:32], r_(b, 16))
                link(dve.tensor_copy(counts_i[:, 32:33], r_(a + 15, 1)))
                link(dve.tensor_scalar(r_(a, 16), r_(b, 16), float(BLOCK), None, ALU.mult))
                link(dve.tensor_tensor(by_tile(R_RP, 16), by_tile(R_POS, 16),
                                       r_(a, 16).unsqueeze(1).to_broadcast([P, nt, 16]), ALU.add))
                for c, hot in enumerate((R_O1, R_O2)):
                    link(dve.tensor_tensor(r_(R_EQ, 16 * nt), r_(R_RP, 16 * nt), r_(hot, 16 * nt), ALU.mult))
                    link(dve.tensor_reduce(r_(R_ROW + 4 * c, nt), by_tile(R_EQ, 16), AX.X, ALU.add))
                for c in range(2):
                    ins = dve.tensor_copy(route_i[:, 4 * c:4 * c + nt], r_(R_ROW + 4 * c, nt))
                ins.then_inc(routed[l], 1)

                dve.wait_ge(routed[l], 1)
                n_all = dve.value_load(counts_i[0:1, 2 * N_EXP:2 * N_EXP + 1], min_val=1, max_val=MAX_BLOCKS)
                dve.wait_ge(hg_in[l], 16)
                dve.tensor_copy(hg[0:BLOCK, :], hg_ring[0:BLOCK, 0:D]).then_inc(hg_ready[l], 1)
                with dve.Fori(0, n_all) as g:
                    dve.wait_ge(hgt_full[l], g + 1)
                    dve.wait_ge(hg_in[l], 16 * (g + 2))
                    dve.sem_inc(dve_steps, 1)
                    dve.tensor_copy(hg[0:BLOCK, :], hg_ring[0:BLOCK, bass.ds(((g + 1) % HG_AHEAD) * D, D)]
                                    ).then_inc(hg_ready[l], 1)
                    for half in range(2):
                        cols = slice(256 * half, 256 * half + 256)
                        dve.wait_ge(sg_ready[l], 2 * g + (half + 1))
                        dve.tensor_tensor(hid[0:BLOCK, cols], sg[0:BLOCK, cols],
                                          bank[(1, 4)[half]][BLOCK:2 * BLOCK, 0:256], ALU.mult).then_inc(hid_ready[l], 1)
                        dve.wait_ge(hidt_full[l], 2 * g + (half + 1))
                        dve.tensor_copy(hidt[:, 2 * half:2 * half + 2, :],
                                        bank[(2, 5)[half]][:, 0:128].rearrange("p (k r) -> p k r", k=2)
                                        ).then_inc(hidt_ready[l], 1)
                    dve.wait_ge(y_full[l], g + 1)
                    dve.wait_ge(y_free[l], g + 1)
                    dve.sem_inc(dve_steps, 1)
                    dve.tensor_copy(y_ring[:, bass.ds((g % Y_BUFS) * 512, 512)], bank[3][:, :]).then_inc(y_ready[l], 1)
                dve.wait_ge(gates_in[l], 16 * 2 * (nt // 2))
                for t in range(nt):
                    y1, y2 = y_in[t % 2]
                    dve.wait_ge(y_back[t % 2][l], 32 * (t // 2 + 1))
                    link(dve.tensor_scalar(y1, y1, wsel[:, 0, t:t + 1], None, ALU.mult))
                    link(dve.scalar_tensor_tensor(y1, y2, wsel[:, 1, t:t + 1], y1, ALU.mult, ALU.add))
                    link(dve.tensor_tensor(y1, y1, rows[:, 0 if t < XT else 1, :], ALU.mult))
                    dve.tensor_tensor(x_res[:, t, :], x_res[:, t, :], y1, ALU.add).then_inc(x_out[l], 1)
            dve.wait_ge(fin_in, 16)
            for t in range(XT):
                norm(None, 32, t, fssq, fin_var, fin_std, rows[:, 2, :], None, h_tok[:, t, :]).then_inc(fin_ready, 1)

        @block.gpsimd
        def _(pool):
            def row(src):
                return src.to_broadcast([P, src.shape[1]])

            consts = [(cst[:, :], io["consts"])]
            for i, n in enumerate(("diff_lambda_q1", "diff_lambda_k1", "diff_lambda_q2", "diff_lambda_k2")):
                consts.append((h_tok[:, 0, 64 * i:64 * i + 64], row(io[n].rearrange("(a l) d -> a (l d)", a=1))))
            for i, n in enumerate(("gqa_q_norm", "gqa_k_norm")):
                for l in range(LAYERS):
                    consts.append((gains[:, l, i, :], row(io[n][l:l + 1, :])))
            consts.append((subg[:, :, :].rearrange("p l d -> p (l d)"),
                           row(io["diff_subln"].rearrange("(a l) d -> a (l d)", a=1))))
            for dst, src in consts:
                pool.dma_start(dst, src).then_inc(consts_in, 16)
            with nc.allow_non_contiguous_dma(reason="twenty biases"):
                pool.dma_start(rbias[:, :, 0:4], io["router_group_b"].rearrange("(a l) g -> a l g", a=1)
                               .to_broadcast([P, LAYERS, 4])).then_inc(consts_in, 16)
                pool.dma_start(rbias[:, :, 4:20], io["router_expert_b"].rearrange("(a l) g -> a l g", a=1)
                               .to_broadcast([P, LAYERS, 16])).then_inc(consts_in, 16)

            rounds = [(0, 0), (0, 1), (0, 2), (1, 0), (1, 1), (1, 2)]

            def chunk_rows(vec, a, b):
                n = (b - a) // 512
                return vec[a:b].rearrange("(j o n) -> j o n", j=n, o=1).to_broadcast([n, 32, 512])

            def mod_round(n):
                l, r = rounds[n]
                if n >= 1:
                    pool.wait_ge(mod_done, n)
                pool.dma_start(mod_add, chunk_rows(io["b_mod"][l], r * 2048, (r + 1) * 2048)).then_inc(mod_b_in, 16)
                pool.wait_ge(mod_sum, n + 1)
                if r == 0:
                    pool.dma_start(mod_add[64:128, :], chunk_rows(io["norm_attn"][l], 0, D)).then_inc(mod_b_in, 16)
                if r == 2:
                    pool.dma_start(mod_add[0:64, :], chunk_rows(io["norm_ffn"][l], 0, D)).then_inc(mod_b_in, 16)
                pool.wait_ge(mod_done, n + 1)
                for c in range(2):
                    pool.dma_start(modd[l, c, r * 2048:(r + 1) * 2048].rearrange("(j n) -> j n", j=4),
                                   mod_row[c:P:32, :]).then_inc(mod_stored, 16)
                pool.wait_ge(mod_stored, 32 * (n + 1))

            def load_row(dst, l, c, sixth, s):
                pool.dma_start(rows[:, dst, :], row(modd[l, c:c + 1, sixth * D:(sixth + 1) * D])).then_inc(s, 16)

            pool.wait_ge(zeroed, 1)
            flat = wind.rearrange("l r h c -> (l r h c)").rearrange("(p n) -> p n", n=256)
            pool.dma_start(flat, zeros[0:flat.shape[0], :]).then_inc(wind_zero, 16)
            pool.wait_ge(wind_zero, 16)
            for l in range(LAYERS):
                pool.dma_start(wind[l, :, :, 48:79], io["na_rpb"][l].rearrange("h r c -> r h c")).then_inc(wind_in, 16)
            mod_round(0)
            load_row(2, 0, 0, 1, ga_in[0][0])
            load_row(3, 0, 0, 0, ga_in[0][0])
            load_row(0, 0, 1, 1, ga_in[1][0])
            load_row(1, 0, 1, 0, ga_in[1][0])
            pool.wait_ge(wind_in, 16 * LAYERS)
            for l in range(LAYERS):
                nt = query_tiles(l)
                pool.wait_ge(h_ready[l], TILES)
                for q in range(2):
                    for half in range(2):
                        r = 2 * q + half
                        a = wind[l, 7 - r:11 - r, :, :]
                        src = bass.AP(a.tensor, a.offset, [[1, 64], [128, 24], [1, 64]])
                        pool.dma_start(win[64 * half:64 * half + 64, q, :, :, :].rearrange("p r h c -> p (r h) c"),
                                       src).then_inc(ga_in[2][l], 16)
                if l == 0:
                    for n in range(1, 6):
                        mod_round(n)
                units = head_units(l)
                last_na = max(u for u, (k, _, _) in enumerate(units) if k == "na")
                full(pool, ("T", l, last_na, 0))
                load_row(0, l, 0, 2, gates_in[l])
                if nt > XT:
                    load_row(1, l, 1, 2, gates_in[l])
                load_row(2, l, 0, 4, ga_in[0][l])
                load_row(3, l, 0, 3, ga_in[0][l])
                full(pool, ("OBt", l, nt - 1))
                if nt > XT:
                    for i, sixth in enumerate((4, 3)):
                        pool.dma_start(next_rows[:, i, :], row(modd[l, 1:2, sixth * D:(sixth + 1) * D])
                                       ).then_inc(ga_in[1][l], 16)
                pool.dma_start(w_route[:, :, 0:4], io["router_group_w"][l].rearrange("(k p) n -> p k n", p=P)
                               ).then_inc(route_w_in[l], 16)
                pool.dma_start(w_route[:, :, 4:20], io["router_expert_w"][l].rearrange("(k p) n -> p k n", p=P)
                               ).then_inc(route_w_in[l], 16)
                pool.wait_ge(x_mid[l], nt)
                load_row(0, l, 0, 5, gates_in[l])
                if nt > XT:
                    load_row(1, l, 1, 5, gates_in[l])
                pool.wait_ge(h2_ready[l], XT)
                if l + 1 < LAYERS:
                    load_row(2, l + 1, 0, 1, ga_in[0][l + 1])
                    load_row(3, l + 1, 0, 0, ga_in[0][l + 1])
                else:
                    pool.dma_start(rows[:, 2, :], row(io["final_norm"].rearrange("(a d) -> a d", a=1))
                                   ).then_inc(fin_in, 16)
                pool.wait_ge(hbuf_zero, 16)
                pool.wait_ge(routed[l], 1)
                for t in range(nt):
                    for c in range(2):
                        pool.indirect_dma_start(
                            out=hbuf, out_offset=bass.IndirectOffsetOnAxis(ap=route_i[:, 4 * c + t:4 * c + t + 1], axis=0),
                            in_=h_tok[:, t, :], in_offset=None).then_inc(scattered[l], 16)
                pool.wait_ge(scattered[l], 32 * nt)
                for g in range(HG_AHEAD):
                    if g:
                        pool.wait_ge(hg_in[l], 16 * g)
                    pool.dma_start(hg_ring[0:BLOCK, g * D:(g + 1) * D], hbuf[g * BLOCK:(g + 1) * BLOCK, :]
                                   ).then_inc(hg_in[l], 16)
                pool.sem_inc(y_free[l], Y_BUFS)
                n_all = pool.value_load(counts_i[0:1, 2 * N_EXP:2 * N_EXP + 1], min_val=1, max_val=MAX_BLOCKS)
                with pool.Fori(0, n_all) as g:
                    pool.wait_ge(y_ready[l], g + 1)
                    for half in range(2):
                        pool.dma_start(hbuf[bass.ds(g * BLOCK, BLOCK), 512 * half:512 * half + 512],
                                       y_ring[64 * half:64 * half + 64, bass.ds((g % Y_BUFS) * 512, 512)]
                                       ).then_inc(y_stored[l], 16)
                    pool.wait_ge(hg_in[l], 16 * (g + HG_AHEAD))
                    pool.dma_start(hg_ring[0:BLOCK, bass.ds((g % HG_AHEAD) * D, D)],
                                   hbuf[bass.ds((g + HG_AHEAD) * BLOCK, BLOCK), :]).then_inc(hg_in[l], 16)
                    pool.wait_ge(y_stored[l], 32 * (g + 1))
                    pool.sem_inc(y_free[l], 1)
                pool.wait_ge(hg_in[l], 16 * (n_all + HG_AHEAD))
                pool.wait_ge(y_stored[l], 32 * n_all)
                pool.sem_inc(pool_steps, 1)
                for t in range(nt):
                    if t >= 2:
                        pool.wait_ge(x_out[l], t - 1)
                    for c in range(2):
                        pool.indirect_dma_start(
                            out=y_in[t % 2][c], out_offset=None, in_=hbuf,
                            in_offset=bass.IndirectOffsetOnAxis(ap=route_i[:, 4 * c + t:4 * c + t + 1], axis=0)
                        ).then_inc(y_back[t % 2][l], 16)
                if l + 1 < LAYERS:
                    pool.wait_ge(x_out[l], XT)
                    load_row(0, l + 1, 1, 1, ga_in[1][l + 1])
                    pool.wait_ge(x_out[l], nt)
                    load_row(1, l + 1, 1, 0, ga_in[1][l + 1])
            for t in range(XT):
                pool.wait_ge(fin_ready, t + 1)
                pool.dma_start(out[0, t * P:(t + 1) * P, :], h_tok[:, t, :]).then_inc(stored, 16)
            pool.wait_ge(stored, 16 * XT)


_INS = ["x", "c", "ctx", "c_ctx", "w_mod", "b_mod", "norm_attn", "norm_ffn", "w_in", "w_out", "na_rpb",
        "diff_lambda_q1", "diff_lambda_k1", "diff_lambda_q2", "diff_lambda_k2", "diff_subln", "gqa_q_norm",
        "gqa_k_norm", "router_group_w", "router_group_b", "router_expert_w", "router_expert_b", "w_gate", "w_up",
        "w_down", "final_norm"]


def kernel(**inputs):
    import numpy as _np
    import concourse.bacc as _bacc
    from concourse import mybir as _mybir
    from concourse.bass_utils import run_bass_kernel_spmd as _run

    nc = _bacc.Bacc("TRN2", target_bir_lowering=False, num_devices=1)
    arrays, io = {}, {}
    for name in _INS + ["consts"]:
        a = constant_table() if name == "consts" else _np.ascontiguousarray(inputs[name])
        arrays[f"in_{name}_dram"] = a
        io[name] = nc.dram_tensor(f"in_{name}_dram", a.shape, _mybir.dt.from_np(a.dtype), kind="ExternalInput").ap()
    out = nc.dram_tensor("out_0_dram", (1, SEQ, D), _mybir.dt.float32, kind="ExternalOutput").ap()
    hybrid_block(nc, io, out)
    r = _run(nc, [arrays], core_ids=[0])
    return r.results[0]["out_0_dram"]
```

```python
import math
from contextlib import ExitStack

import numpy as np

import concourse.bass as bass
from concourse import mybir

P = 128
F32 = mybir.dt.float32
I32 = mybir.dt.int32
ALU = mybir.AluOpType
ACT = mybir.ActivationFunctionType
AX = mybir.AxisListType

D = 1024
KD = D // P
SEQ = 256
CTX = 256
GRID_W = 64
LAYERS = 2
IN_W = 2560
HID = 512
N_EXP = 16
N_GRP = 4
N_TOK = SEQ + CTX
TILES = N_TOK // P
XT = SEQ // P
EPS = 1e-6
BIG = 1e30
BLOCK = 64
SLOTS = 6
SLOT_W = 4096
HG_AHEAD = 4
Y_BUFS = 4
MAX_BLOCKS = 2 * N_TOK // BLOCK + N_EXP

C_ID, C_TRI, C_ONE, C_IG, C_IE, C_THR, C_C16, C_S16, C_C32, C_S32, C_MASK, C_FLIP, C_END = np.cumsum(
    [0, P, P, 1, N_GRP, N_EXP, 7, 64, 64, 128, 128, 64, P]).tolist()


def constant_table():
    t = np.zeros((P, C_END), np.float32)
    t[:, C_ID:C_ID + P] = np.eye(P)
    t[:, C_TRI:C_TRI + P] = np.triu(np.ones((P, P)), 1)
    t[:, C_ONE] = 1.0
    t[:, C_IG:C_IG + N_GRP] = np.arange(N_GRP) - N_GRP
    t[:, C_IE:C_IE + N_EXP] = np.arange(N_EXP) - N_EXP
    t[:, C_THR:C_THR + 7] = BLOCK * np.arange(1, 8)
    for dim, cc, ss in ((32, C_C16, C_S16), (64, C_C32, C_S32)):
        tok = np.arange(SEQ)
        freqs = (np.float32(10000.0) ** (-np.arange(dim // 4, dtype=np.float32) / np.float32(dim // 4)))
        ang = np.concatenate([(tok // GRID_W).astype(np.float32)[:, None] * freqs,
                              (tok % GRID_W).astype(np.float32)[:, None] * freqs], -1)
        cos, sin = np.cos(ang), np.sin(ang)
        for i in range(XT):
            rows = slice(i * P, (i + 1) * P)
            t[:, cc + dim * i:cc + dim * (i + 1)] = np.concatenate([cos[rows], cos[rows]], -1)
            t[:, ss + dim * i:ss + dim * (i + 1)] = np.concatenate([-sin[rows], sin[rows]], -1)
    col = np.arange(GRID_W)
    start = np.clip(col - 8, 0, GRID_W - 16)[:, None]
    inside = (col[None] >= start) & (col[None] < start + 16)
    t[:, C_MASK:C_MASK + 64] = np.tile(np.where(inside, 0.0, -BIG)[::-1], (2, 1))
    t[:, C_FLIP:C_FLIP + P] = np.kron(np.eye(2), np.eye(GRID_W)[::-1])
    return t


GROUPS = {"F": [(1920, 2432)], "D": [(1152, 1664)], "A": [(0, 384)], "B": [(384, 768)], "C": [(768, 1152)],
          "E": [(1664, 1920), (2432, 2560)]}


def query_tiles(l):
    return TILES if l < LAYERS - 1 else XT


def head_units(l):
    sides = (True, False) if l < LAYERS - 1 else (True,)
    return [(k, h, x) for k, n in (("na", 6), ("diff", 4), ("gqa", 6)) for h in range(n) for x in sides]


def sub_norm_unit(l):
    return max(u for u, (k, _, _) in enumerate(head_units(l)) if k == "diff") + 3


def in_products(l):
    out = [("F", l, t) for t in range(TILES)] + [("D", l, t) for t in range(TILES)]
    out += [("Ft", l, t) for t in range(TILES)] + [("A", l, m) for m in range(3)]
    out += [("Dt", l, t) for t in range(TILES)] + [("B", l, m) for m in range(3)]
    out += [("C", l, t) for t in range(TILES)] + [("E", l, t) for t in range(TILES)]
    return out


LAYER_START = [(0, "tr1"), (1, "tr1"), (0, "F"), (2, "tr1"), (1, "F"), (3, "tr1"), (2, "F"), (3, "F")]

MOD_LATER = [(0, r, k) for r in (1, 2) for k in range(4)] + [(1, r, k) for r in range(3) for k in range(4)]


def mod_pieces_after(place):
    kind, n = place
    if kind == "in":
        ks = [i for i, p in enumerate(in_products(0)) if p[0] in "DABCE" and len(p[0]) == 1][::2]
        i = ks.index(n) if n in ks else None
    else:
        i = 9 + n // 3 if n % 3 == 0 else None
    return [] if i is None or i >= len(MOD_LATER) else [MOD_LATER[i]]


def psum_products():
    order = []
    turn = [0]

    def rotate(key):
        order.append((key, turn[0] % 6))
        turn[0] += 1

    def mods(place):
        for l, r, k in mod_pieces_after(place):
            if (r, k) == (1, 0) and l > 0:
                order.append((("modT", l), 7))
            if k == 3:
                order.append((("mod", l, r), 7))

    order.append((("mod", 0, 0), 7))
    for l in range(LAYERS):
        for t, what in LAYER_START:
            if what == "tr1":
                for half in range(2):
                    rotate(("tr1", l, t, half))
            else:
                if t == 0 and l == 0:
                    order.append((("modT", 0), 7))
                rotate(("F", l, t))
        for n, key in enumerate(in_products(l)):
            if key[0] != "F":
                rotate(key)
            if l == 0:
                mods(("in", n))
        units = head_units(l)

        def scores(u):
            kind, h, x = units[u]
            if kind == "diff":
                sets = [(0, 0), (1, 2)]
            else:
                sets = [(0, 2 * (u % 2))]
            for s, b in sets:
                for q in range(2 if x else 1):
                    order.append((("S", l, u, s, q), b + q))

        scores(0)
        for u in range(len(units) + 1):
            if u + 1 < len(units):
                scores(u + 1)
            if u < len(units):
                if units[u][2]:
                    order.append((("T", l, u, 0), 4))
                    order.append((("T", l, u, 1), 5))
                else:
                    order.append((("T", l, u, 0), 4 + u % 2))
            if u >= 1:
                order.append((("O", l, u - 1), 6))
            if u == sub_norm_unit(l):
                for pair in range(query_tiles(l) // 2):
                    order.append((("OBt", l, pair), 6))
            if l == 0:
                mods(("unit", u))
        turn[0] = 0
        for t in range(query_tiles(l) + 1):
            if t < query_tiles(l):
                for half in range(2):
                    rotate(("Y", l, t, half))
            if t == 2:
                order.append((("R", l), 6))
            if t >= 1:
                for half in range(2):
                    rotate(("tr2", l, t - 1, half))
        order.append((("cum", l), 7))
        turn[0] = 0
    place, count = {}, [0] * 8
    last = {}
    before = {}
    for key, b in order:
        place[key] = (b, count[b])
        count[b] += 1
        before[key] = last.get(b)
        last[b] = key
    return place, before, [k for k, _ in order]


PLACE, BEFORE, ORDER = psum_products()


def ring_plan():
    items = [("mod", 0, 0, k) for k in range(4)]
    for l in range(LAYERS):
        seen = set()
        for n, p in enumerate(in_products(l)):
            if p[0] in GROUPS and p[0] not in seen:
                seen.add(p[0])
                items.append(("in", l, p[0]))
            if l == 0:
                items += [("mod", *m) for m in mod_pieces_after(("in", n))]
        if l == 0:
            for u in range(len(head_units(0)) + 1):
                items += [("mod", *m) for m in mod_pieces_after(("unit", u))]
        items += [("out", l, 0), ("out", l, 1), ("exp", l)]
    plan, n = [], 0
    for it in items:
        plan.append((it, n % SLOTS))
        n += 3 * N_EXP if it[0] == "exp" else 1
    return plan


RING = ring_plan()


def hybrid_block(nc, io, out):
    place, before = PLACE, BEFORE
    with ExitStack() as ctx:
        def sb(name, shape, dt=F32):
            return ctx.enter_context(nc.sbuf_tensor(name, shape, dt))

        def sem(name):
            return ctx.enter_context(nc.semaphore(name))

        def sems(name):
            return [sem(f"{name}_{l}") for l in range(LAYERS)]

        ring = sb("ring", [P, SLOTS, SLOT_W])
        x_res = sb("x_res", [P, TILES, D])
        h_tok = sb("h_tok", [P, TILES, D])
        h_t = sb("h_t", [P, KD, N_TOK])
        rows = sb("rows", [P, 4, D])
        big = sb("big", [P, 10240])
        cst = sb("cst", [P, C_END])
        gains = sb("gains", [P, LAYERS, 2, 64])
        subg = sb("subg", [P, LAYERS, 64])
        rbias = sb("rbias", [P, LAYERS, N_GRP + N_EXP])
        zeros = sb("zeros", [P, 128])
        cond = sb("cond", [P, KD, 2])
        csil = sb("csil", [P, KD, 16, 2])
        stat = sb("stat", [P, 80])
        fstat = sb("fstat", [P, 3, 8])
        neglam = sb("neglam", [P, LAYERS])
        modcol = sb("modcol", [P, LAYERS, 2, 2 * KD])

        ident = cst[:, C_ID:C_ID + P]
        bank = [ctx.enter_context(nc.psum_tensor(f"bank{i}", [P, 512], F32)) for i in range(8)]

        qk = big[:, 0:7168].rearrange("p (c t) -> p c t", t=N_TOK)
        Q_NA, K_NA, Q_DF, K_DF, Q_GQ, K_GQ = 0, 3, 6, 8, 10, 13
        v_tok = big[:, 7168:10240].rearrange("p (t c) -> p t c", t=TILES)
        ob = big[:, 0:1024].rearrange("p (t c) -> p t c", t=TILES)
        ob_sq = big[:, 1024:2048]
        win = rows[:, 0:3, :].rearrange("p a b -> p (a b)").rearrange("p (q r h c) -> p q r h c", q=2, r=4, h=6)
        mod_row = rows[:, 3, 0:512]
        mod_add = rows[:, 3, 512:1024]
        gain_first = rows[64:128, 2, 0:512]
        lam_in = rows[:, 0, 0:384]
        prob = [h_tok[:, i, :].rearrange("p (q k) -> p q k", q=2) for i in range(2)]
        prob_t = [h_tok[:, 2 + i, :].rearrange("p (k q) -> p k q", k=4) for i in range(2)]
        mixed = h_t

        o = 0

        def carve(n):
            nonlocal o
            o += n
            return big[:, o - n:o]

        w_route = carve(KD * 20).rearrange("p (k n) -> p k n", k=KD)
        y_in = [[carve(1024) for _ in range(2)] for _ in range(2)]
        hg_ring = big[:, o - HG_AHEAD * D:o]
        hg = carve(1024)
        hgt = carve(512).rearrange("p (k r) -> p k r", k=KD)
        sg = carve(512)
        hid = carve(512)
        hidt = carve(256).rearrange("p (k r) -> p k r", k=4)
        y_ring = carve(Y_BUFS * 512)
        lg = carve(80)
        rt = carve(1008)
        next_rows = big[:, 2048:4096].rearrange("p (a d) -> p a d", a=2)
        route_i = sb("route_i", [P, 2 * TILES], I32)
        counts_i = sb("counts_i", [P, 3 * N_EXP + 1], I32)
        wsel = sb("wsel", [P, 2, TILES])

        modd = nc.dram_tensor("modd", [LAYERS, 2, 6 * D], F32).ap()
        wind = nc.dram_tensor("wind", [LAYERS, 15, 6, 128], F32).ap()
        hbuf = nc.dram_tensor("hbuf", [(MAX_BLOCKS + HG_AHEAD) * BLOCK, D], F32).ap()

        bank_full = [sem(f"bank_full{b}") for b in range(8)]
        bank_read = [sem(f"bank_read{b}") for b in range(8)]
        slot_in = [sem(f"slot_in{s}") for s in range(SLOTS)]
        mod_piece = sem("mod_piece")
        consts_in = sem("consts_in")
        cond_in = sem("cond_in")
        table_in = sem("table_in")
        x_in = sem("x_in")
        ctx_in = sem("ctx_in")
        mod_first_in = sem("mod_first_in")
        csil_ready = sem("csil_ready")
        zeroed = sem("zeroed")
        wind_zero = sem("wind_zero")
        wind_in = sem("wind_in")
        hbuf_zero = sem("hbuf_zero")
        dve_order = sem("dve_order")
        act_order = sem("act_order")
        lam_dots = sem("lam_dots")
        lam_exp = sem("lam_exp")
        mod_b_in = sem("mod_b_in")
        mod_sum = sem("mod_sum")
        mod_done = sem("mod_done")
        mod_stored = sem("mod_stored")
        ga_in = [sems(f"rows{i}_in") for i in range(3)]
        ssq = sems("ssq")
        var = sems("var")
        std = sems("std")
        h_ready = sems("h_ready")
        fsq = sems("fsq")
        fvar = sems("fvar")
        fstd = sems("fstd")
        rope_ready = sems("rope_ready")
        ctx_copied = sems("ctx_copied")
        win_ready = sems("win_ready")
        max_ready = sems("max_ready")
        exp_ready = sems("exp_ready")
        probs_ready = sems("probs_ready")
        sub_var = sems("sub_var")
        sub_std = sems("sub_std")
        sub_ready = sems("sub_ready")
        x_mid = sems("x_mid")
        ssq2 = sems("ssq2")
        var2 = sems("var2")
        std2 = sems("std2")
        h2_ready = sems("h2_ready")
        route_w_in = sems("route_w_in")
        pick_ready = sems("pick_ready")
        gexp_in = sems("gexp_in")
        gexp = sems("gexp")
        routed = sems("routed")
        scattered = sems("scattered")
        gates_in = sems("gates_in")
        hg_in = sems("hg_in")
        hg_ready = sems("hg_ready")
        hgt_full = sems("hgt_full")
        hgt_ready = sems("hgt_ready")
        gu_full = sems("gu_full")
        sg_ready = sems("sg_ready")
        hid_ready = sems("hid_ready")
        hidt_full = sems("hidt_full")
        hidt_ready = sems("hidt_ready")
        y_full = sems("y_full")
        y_ready = sems("y_ready")
        y_stored = sems("y_stored")
        y_free = sems("y_free")
        y_back = [sems(f"y_back{i}") for i in range(2)]
        x_out = sems("x_out")
        fin_in = sem("fin_in")
        fssq = sem("fssq")
        fin_var = sem("fin_var")
        fin_std = sem("fin_std")
        fin_ready = sem("fin_ready")
        stored = sem("stored")
        pe_steps = sem("pe_steps")
        pool_steps = sem("pool_steps")
        dve_steps = sem("dve_steps")

        def full(eng, key):
            b, n = place[key]
            eng.wait_ge(bank_full[b], n + 1)

        def emptied(eng, key):
            b, n = place[key]
            eng.wait_ge(bank_read[b], n + 1)

        def ps(key):
            return bank[place[key][0]]

        def read_sem(key):
            return bank_read[place[key][0]]

        def last_product(l, item):
            if item[0] == "mod":
                return ("mod", item[1], item[2])
            if item[0] == "in":
                return [p for p in in_products(item[1]) if p[0] == item[2]][-1]
            return ("Y", item[1], query_tiles(item[1]) - 1, 1)

        fills = [0] * SLOTS
        slot_before, holder, load_waits = {}, [None] * SLOTS, {}
        pieces = 0
        for item, s in RING:
            if item[0] == "exp":
                slot_before[item] = [(s + j) % SLOTS for j in range(SLOTS)], list(fills)
                load_waits[item] = [holder[(s + j) % SLOTS] for j in range(SLOTS)]
                for j in range(SLOTS):
                    fills[j] += N_EXP // 2
                    holder[(s + j) % SLOTS] = ("exp", item[1], j)
                continue
            load_waits[item] = holder[s]
            fills[s] += 2 if item[0] == "in" and item[2] == "E" else 1
            slot_before[item] = s, fills[s]
            if item[0] == "mod" and item[3] < 3:
                pieces += 1
                holder[s] = ("piece", pieces)
            else:
                holder[s] = ("product", last_product(None, item))

        def wait_free(eng, h):
            if h is None:
                return
            if h[0] == "piece":
                eng.wait_ge(mod_piece, h[1])
            elif h[0] == "product":
                full(eng, h[1])
            else:
                end = eng.value_load(counts_i[0:1, 3 * N_EXP - 2 + h[2] // 3:3 * N_EXP - 1 + h[2] // 3], min_val=1,
                                     max_val=MAX_BLOCKS)
                if h[2] % 3 < 2:
                    eng.wait_ge(gu_full[h[1]], 2 * end)
                else:
                    eng.wait_ge(y_full[h[1]], end)

        def landed(eng, item):
            s, n = slot_before[item]
            eng.wait_ge(slot_in[s], 16 * n)
            return ring[:, s, :]

        def mix_half(kind, h):
            return h % 2

        def mix_chunk(kind, h):
            return {"na": 0, "gqa": 5}[kind] + h // 2

        def maxes(l, u, s):
            return sum(2 if k == "diff" else 1 for k, _, _ in head_units(l)[:u]) + s + 1

        R_M = 0
        R_GD, R_GE, R_C4, R_OG, R_PEN = 64, 80, 96, 112, 128
        R_E1, R_EQ, R_C16, R_O1, R_O2, R_X = 144, 208, 272, 336, 400, 464
        R_GM, R_GS, R_PG, R_CI, R_M1, R_I1, R_M2, R_I2, R_DM, R_E2, R_DEN, R_R = [528 + 4 * i for i in range(12)]
        R_TOT, R_CMP, R_NB, R_PA, R_PB = 576, 640, 752, 768, 784
        R_POS, R_RP, R_ROW, R_LOC = 800, 864, 928, 944

        def mod_loads(n, second):
            done_ = sum(1 if r == 1 else 2 for _, r in ROUNDS[1:n])
            return done_ + 1 + second

        ROUNDS = [(l, r) for l in range(LAYERS) for r in range(3)]

        def mod_stores(n):
            return sum(r > 0 for _, r in ROUNDS[:n])

        N_CONST = 11

        def chunk_rows(vec, a, b):
            n = (b - a) // 512
            return vec[a:b].rearrange("(j o n) -> j o n", j=n, o=1).to_broadcast([n, 32, 512])

        block = ctx.enter_context(nc.Block())

        @block.sync
        def _(sp):
            def load_item(item):
                s, _ = slot_before[item]
                wait_free(sp, load_waits[item])
                if item[0] == "mod":
                    _, l, r, k = item
                    src = io["w_mod"][l, k * 256:(k + 1) * 256, r * 2048:(r + 1) * 2048]
                    sp.dma_start(ring[:, s, :].rearrange("p (a n) -> p a n", a=2),
                                 src.rearrange("(a p) n -> p a n", p=P)).then_inc(slot_in[s], 16)
                elif item[0] == "in":
                    _, l, g = item
                    width = sum(b - a for a, b in GROUPS[g])
                    dst = ring[:, s, 0:KD * width].rearrange("p (k n) -> p k n", k=KD)
                    at = 0
                    for a, b in GROUPS[g]:
                        sp.dma_start(dst[:, :, at:at + b - a],
                                     io["w_in"][l, :, a:b].rearrange("(k p) n -> p k n", p=P)).then_inc(slot_in[s], 16)
                        at += b - a
                else:
                    _, l, half = item
                    sp.dma_start(ring[:, s, :].rearrange("p (k n) -> p k n", k=4),
                                 io["w_out"][l, half * 512:(half + 1) * 512, :].rearrange("(k p) n -> p k n", p=P)
                                 ).then_inc(slot_in[s], 16)

            def load_expert(l, e, slots, end):
                for j, (w, k) in enumerate((("w_gate", 8), ("w_up", 8), ("w_down", 4))):
                    if j == 0:
                        sp.wait_ge(gu_full[l], 2 * end)
                    if j == 2:
                        sp.wait_ge(y_full[l], end)
                    dst = ring[:, slots[j], :].rearrange("p (k n) -> p k n", k=k)
                    src = io[w][l, bass.ds(e, 1), :, :].rearrange("e (k p) n -> p (e k) n", p=P)
                    sp.dma_start(dst, src).then_inc(slot_in[slots[j]], 16)

            sp.dma_start(cond[:, :, 0], io["c"][0, :].rearrange("(k p) -> p k", p=P),
                         allow_slow_non_contiguous=True).then_inc(cond_in, 16)
            sp.dma_start(cond[:, :, 1], io["c_ctx"].rearrange("(k p) -> p k", p=P),
                         allow_slow_non_contiguous=True).then_inc(cond_in, 16)
            sp.dma_start(cst[:, :], io["consts"]).then_inc(table_in, 16)
            sp.dma_start(mod_add, chunk_rows(io["b_mod"][0], 0, 2048)).then_inc(mod_first_in, 16)
            sp.dma_start(gain_first, chunk_rows(io["norm_attn"][0], 0, D)).then_inc(mod_first_in, 16)
            for item, _ in RING[:2]:
                load_item(item)
            sp.dma_start(x_res[:, 0:XT, :], io["x"][0].rearrange("(t p) d -> p t d", p=P)).then_inc(x_in, 16)
            for item, _ in RING[2:5]:
                load_item(item)
            sp.dma_start(x_res[:, XT:, :], io["ctx"][0].rearrange("(t p) d -> p t d", p=P)).then_inc(ctx_in, 16)
            for item, _ in RING[5:]:
                if item[0] != "exp":
                    if item[:2] == ("in", 1) and item[2] != "F":
                        sp.wait_ge(y_back[(query_tiles(0) - 1) % 2][0], 32 * (query_tiles(0) // 2))
                    load_item(item)
                    if item == ("in", 0, "A"):
                        sp.wait_ge(zeroed, 1)
                        sp.dma_start(hbuf.rearrange("(p a) (b n) -> p (a b) n", p=P // 2, n=128),
                                     zeros[0:P // 2, :].unsqueeze(1).to_broadcast(
                                         [P // 2, (MAX_BLOCKS + HG_AHEAD) * 8, 128])).then_inc(hbuf_zero, 16)
                    continue
                l = item[1]
                slots, _ = slot_before[item]
                for j in range(SLOTS):
                    wait_free(sp, load_waits[item][j])
                    w, k = (("w_gate", 8), ("w_up", 8), ("w_down", 4))[j % 3]
                    sp.dma_start(ring[:, slots[j], :].rearrange("p (k n) -> p k n", k=k),
                                 io[w][l, j // 3].rearrange("(k p) n -> p k n", p=P)).then_inc(slot_in[slots[j]], 16)
                sp.wait_ge(routed[l], 1)
                with sp.Fori(1, N_EXP // 2) as pair:
                    for u in range(2):
                        end = sp.value_load(counts_i[0:1, bass.ds(2 * pair + (2 * N_EXP - 2 + u), 1)], min_val=1,
                                            max_val=MAX_BLOCKS)
                        load_expert(l, 2 * pair + u, slots[3 * u:3 * u + 3], end)

        @block.tensor
        def _(pe):
            made = []

            def start(key):
                made.append(key)
                if before[key] is not None:
                    emptied(pe, before[key])
                return ps(key)

            def done(ins, key):
                ins.then_inc(bank_full[place[key][0]], 1)

            def mod(l, r, k):
                w = landed(pe, ("mod", l, r, k)).rearrange("p (a n) -> p a n", a=2)
                key = ("mod", l, r)
                if k == 0 and before[key] is not None:
                    emptied(pe, before[key])
                for a in range(2):
                    lhs = csil[:, 2 * k + a, :, :].rearrange("p o c -> p (o c)")
                    for j in range(4):
                        mm = pe.matmul(bank[7][32 * j:32 * j + 32, :], lhs, w[:, a, 512 * j:512 * j + 512],
                                       start=(k == 0 and a == 0), stop=(k == 3 and a == 1), tile_position=(0, 32 * j))
                if k == 3:
                    made.append(key)
                    done(mm, key)
                else:
                    mm.then_inc(mod_piece, 1)

            def mods(at):
                for m in mod_pieces_after(at):
                    if m[1:] == (1, 0) and m[0] > 0:
                        turn_mod(m[0])
                    mod(*m)

            def transposes(key, src, chunks, rows_in=P):
                dst = start(key)
                for c in range(chunks):
                    mm = pe.transpose(dst[:, c * P:c * P + rows_in], src[:, c * P:(c + 1) * P], ident[0:rows_in, 0:rows_in])
                done(mm, key)

            def turn_mod(l):
                pe.wait_ge(mod_done, ROUNDS.index((l, 0)) + 1)
                transposes(("modT", l), mod_row, 4)

            def in_product(key):
                kind, l, i = key
                nq = P * query_tiles(l)
                if kind == "F" or kind == "D" or kind == "C" or kind == "E":
                    w = landed(pe, ("in", l, kind))
                    n = sum(b - a for a, b in GROUPS[kind])
                    w = w[:, 0:KD * n].rearrange("p (k n) -> p k n", k=KD)
                    lo = 0
                    if i * P >= nq and kind in "FD":
                        lo = 384 if kind == "F" else 256
                    dst = start(key)
                    for k in range(KD):
                        mm = pe.matmul(dst[:, lo:n], h_t[:, k, i * P:(i + 1) * P], w[:, k, lo:n],
                                       start=(k == 0), stop=(k == KD - 1))
                    done(mm, key)
                elif kind in "AB":
                    w = landed(pe, ("in", l, kind))[:, 0:KD * 384].rearrange("p (k n) -> p k n", k=KD)
                    n = nq if kind == "A" else N_TOK
                    dst = start(key)
                    for k in range(KD):
                        mm = pe.matmul(dst[:, 0:n], w[:, k, i * P:(i + 1) * P], h_t[:, k, 0:n],
                                       start=(k == 0), stop=(k == KD - 1))
                    done(mm, key)
                elif kind == "Ft":
                    pe.wait_ge(rope_ready[l], i + 1)
                    lo = 0 if i * P < nq else 3
                    dst = start(key)
                    for c in range(lo, 4):
                        mm = pe.transpose(dst[:, c * P:(c + 1) * P], h_tok[:, i, c * P:(c + 1) * P], ident)
                    done(mm, key)
                else:
                    if i < XT:
                        pe.wait_ge(rope_ready[l], TILES + i + 1)
                    else:
                        pe.wait_ge(ctx_copied[l], i - XT + 1)
                    lo = 0 if i * P < nq else 2
                    dst = start(key)
                    for c in range(lo, 4):
                        mm = pe.transpose(dst[:, c * P:(c + 1) * P], h_tok[:, i, c * P:(c + 1) * P], ident)
                    done(mm, key)

            def scores(l, u):
                kind, h, x = head_units(l)[u]
                sets = 2 if kind == "diff" else 1
                n_k = N_TOK if x else CTX
                k0 = 0 if x else SEQ
                q0 = 0 if x else SEQ
                for s in range(sets):
                    if kind == "na":
                        qi, ki, qp, kp, w = Q_NA + h // 2, K_NA + h // 2, 64 * (h % 2), 64 * (h % 2), 64
                    elif kind == "gqa":
                        qi, ki, qp, kp, w = Q_GQ + h % 3, K_GQ, 64 * (h // 3), 64 * (h // 3), 64
                    else:
                        qi, ki, qp, kp, w = Q_DF + h // 2, K_DF + h // 2, 64 * (h % 2) + 32 * s, 64 * (h % 2) + 32 * s, 32
                    for q in range(2):
                        if x:
                            dst = start(("S", l, u, s, q))
                        elif q == 0:
                            dst = start(("S", l, u, s, 0))
                        if x and kind == "na" and h == 0:
                            pe.wait_ge(win_ready[l], 1)
                        o_ps = dst[:, 0:n_k] if x else dst[:, q * CTX:(q + 1) * CTX]
                        bias = x and kind == "na"
                        mm = pe.matmul(o_ps, qk[qp:qp + w, qi, q0 + q * P:q0 + (q + 1) * P],
                                       qk[kp:kp + w, ki, k0:k0 + n_k], start=True, stop=not bias,
                                       tile_position=(qp, 0))
                        if bias:
                            mm = pe.matmul(dst[:, 0:SEQ], cst[:, C_FLIP:C_FLIP + P], win[:, q, :, h, :], start=False, stop=True)
                        if x:
                            done(mm, ("S", l, u, s, q))
                        elif q == 1:
                            done(mm, ("S", l, u, s, 0))

            def turn_probs(l, u):
                kind, h, x = head_units(l)[u]
                pe.wait_ge(probs_ready[l], u + 1)
                p = prob[0] if kind == "diff" else prob[u % 2]
                if x:
                    for q in range(2):
                        transposes(("T", l, u, q), p[:, q, :], 4)
                else:
                    dst = start(("T", l, u, 0))
                    for kt in range(2):
                        for q in range(2):
                            mm = pe.transpose(dst[:, (2 * kt + q) * P:(2 * kt + q + 1) * P],
                                              p[:, q, kt * P:(kt + 1) * P], ident)
                    done(mm, ("T", l, u, 0))

            def weigh(l, u):
                kind, h, x = head_units(l)[u]
                for q in range(2 if x else 1):
                    emptied(pe, ("T", l, u, q))
                pt = prob_t[u % 2]
                kts = 4 if x else 2
                v0 = {"na": 64 * h, "diff": 384 + 64 * h, "gqa": 640 + 64 * (h // 3)}[kind]
                t0 = 0 if x else XT
                dst = start(("O", l, u))
                if kind == "diff":
                    for q in range(2):
                        for kt in range(kts):
                            mm = pe.matmul(dst[:, 64 * q:64 * q + 64], pt[:, kt, q * P:(q + 1) * P],
                                           v_tok[:, t0 + kt, v0:v0 + 64], start=(kt == 0), stop=(kt == kts - 1))
                else:
                    half = mix_half(kind, h)
                    for kt in range(kts):
                        mm = pe.matmul(dst[64 * half:64 * half + 64, 0:SEQ], v_tok[:, t0 + kt, v0:v0 + 64],
                                       pt[:, kt, :], start=(kt == 0), stop=(kt == kts - 1),
                                       tile_position=(0, 64 * half))
                done(mm, ("O", l, u))

            def out_product(l, t):
                for half in range(2):
                    key = ("Y", l, t, half)
                    dst = start(key)
                    for k in range(KD):
                        w = landed(pe, ("out", l, k // 4)).rearrange("p (k n) -> p k n", k=4)
                        mm = pe.matmul(dst[:, :], mixed[:, k, t * P:(t + 1) * P], w[:, k % 4, half * 512:half * 512 + 512],
                                       start=(k == 0), stop=(k == KD - 1))
                    done(mm, key)

            def experts(l):
                slots, filled = slot_before[("exp", l)]
                t_bank, gu, ht, yb = bank[0], (bank[1], bank[4]), (bank[2], bank[5]), bank[3]

                def turn_rows(g):
                    pe.wait_ge(hg_ready[l], g + 1)
                    pe.sem_inc(pe_steps, 1)
                    for k in range(KD):
                        mm = pe.transpose(t_bank[:, k * BLOCK:(k + 1) * BLOCK], hg[0:BLOCK, k * P:(k + 1) * P],
                                          ident[0:BLOCK, 0:BLOCK])
                    mm.then_inc(hgt_full[l], 1)

                def turn_hidden(g, half):
                    pe.wait_ge(hid_ready[l], 2 * g + (half + 1))
                    pe.sem_inc(pe_steps, 1)
                    for k in range(2):
                        c = 2 * half + k
                        mm = pe.transpose(ht[half][:, k * BLOCK:(k + 1) * BLOCK], hid[0:BLOCK, c * P:(c + 1) * P],
                                          ident[0:BLOCK, 0:BLOCK])
                    mm.then_inc(hidt_full[l], 1)

                for b in range(6):
                    last = [k for k in made if place[k][0] == b][-1]
                    emptied(pe, last)
                pe.wait_ge(routed[l], 1)
                turn_rows(0)
                with pe.Fori(0, N_EXP // 2) as pair:
                    for u in range(2):
                        n_blocks = pe.value_load(counts_i[0:1, bass.ds(2 * pair + u, 1)], min_val=1, max_val=8)
                        first = pe.value_load(counts_i[0:1, bass.ds(2 * pair + (N_EXP + u), 1)], min_val=0,
                                              max_val=MAX_BLOCKS)
                        wg, wu = [ring[:, slots[3 * u + j], :].rearrange("p (k n) -> p k n", k=8) for j in range(2)]
                        wd = ring[:, slots[3 * u + 2], :].rearrange("p (k n) -> p k n", k=4)
                        with pe.Fori(0, n_blocks) as i:
                            g = first + i
                            for j in range(2):
                                s = slots[3 * u + j]
                                pe.wait_ge(slot_in[s], 16 * pair + 16 * (filled[s] + 1))
                            pe.wait_ge(hgt_ready[l], g + 1)
                            for half in range(2):
                                cols = slice(256 * half, 256 * half + 256)
                                for k in range(KD):
                                    pe.matmul(gu[half][0:64, 0:256], hgt[:, k, :], wg[:, k, cols], start=(k == 0),
                                              stop=(k == KD - 1), tile_position=(0, 0))
                                    mm = pe.matmul(gu[half][64:128, 0:256], hgt[:, k, :], wu[:, k, cols],
                                                   start=(k == 0), stop=(k == KD - 1), tile_position=(0, 64))
                                mm.then_inc(gu_full[l], 1)
                            turn_hidden(g, 0)
                            turn_rows(g + 1)
                            turn_hidden(g, 1)
                            s = slots[3 * u + 2]
                            pe.wait_ge(slot_in[s], 16 * pair + 16 * (filled[s] + 1))
                            for half in range(2):
                                pe.wait_ge(hidt_ready[l], 2 * g + (half + 1))
                                for k in range(2 * half, 2 * half + 2):
                                    pe.matmul(yb[0:64, :], hidt[:, k, :], wd[:, k, 0:512], start=(k == 0),
                                              stop=(k == 3), tile_position=(0, 0))
                                    mm = pe.matmul(yb[64:128, :], hidt[:, k, :], wd[:, k, 512:1024], start=(k == 0),
                                                   stop=(k == 3), tile_position=(0, 64))
                            mm.then_inc(y_full[l], 1)
                n_all = pe.value_load(counts_i[0:1, 3 * N_EXP:3 * N_EXP + 1], min_val=1, max_val=MAX_BLOCKS)
                pe.wait_ge(y_ready[l], n_all)
                pe.wait_ge(hgt_ready[l], n_all + 1)

            pe.wait_ge(csil_ready, 1)
            for k in range(4):
                mod(0, 0, k)
            pe.wait_ge(table_in, 16)
            for l in range(LAYERS):
                for t, what in LAYER_START:
                    if what == "tr1":
                        pe.wait_ge(h_ready[l], t + 1)
                        for half in range(2):
                            transposes(("tr1", l, t, half), h_tok[:, t, half * 512:(half + 1) * 512], 4)
                    else:
                        if t == 0 and l == 0:
                            turn_mod(0)
                        for half in range(2):
                            emptied(pe, ("tr1", l, t, half))
                        in_product(("F", l, t))
                for n, key in enumerate(in_products(l)):
                    if key[0] != "F":
                        in_product(key)
                    if l == 0:
                        mods(("in", n))
                for key in in_products(l):
                    if key[0] in ("A", "B", "C", "E", "Ft", "Dt"):
                        emptied(pe, key)
                units = head_units(l)
                scores(l, 0)
                for u in range(len(units) + 1):
                    if u + 1 < len(units):
                        scores(l, u + 1)
                    if u < len(units):
                        turn_probs(l, u)
                    if u >= 1:
                        weigh(l, u - 1)
                    if u == sub_norm_unit(l):
                        pe.wait_ge(sub_ready[l], 1)
                        for pair in range(query_tiles(l) // 2):
                            transposes(("OBt", l, pair), ob[:, 2 * pair:2 * pair + 2, :].rearrange("p t c -> p (t c)"), 4)
                    if l == 0:
                        mods(("unit", u))
                emptied(pe, ("O", l, len(units) - 1))
                for pair in range(query_tiles(l) // 2):
                    emptied(pe, ("OBt", l, pair))
                nt = query_tiles(l)

                def router(t):
                    for half in range(2):
                        emptied(pe, ("tr2", l, t, half))
                    if t == 0:
                        pe.wait_ge(route_w_in[l], 32)
                        start(("R", l))
                    for k in range(KD):
                        mm = pe.matmul(ps(("R", l))[:, 20 * t:20 * t + 20], h_t[:, k, t * P:(t + 1) * P],
                                       w_route[:, k, :], start=(k == 0), stop=(k == KD - 1))
                    if t == nt - 1:
                        done(mm, ("R", l))

                for t in range(nt + 1):
                    if t < nt:
                        out_product(l, t)
                    if t >= 2:
                        router(t - 2)
                    if t >= 1:
                        pe.wait_ge(h2_ready[l], t)
                        for half in range(2):
                            transposes(("tr2", l, t - 1, half), h_tok[:, t - 1, half * 512:(half + 1) * 512], 4)
                router(nt - 1)
                pe.wait_ge(pick_ready[l], 1)
                dst = start(("cum", l))
                picked = rt[:, 0:16 * nt]
                pe.matmul(dst[:, 0:16 * nt], cst[:, C_TRI:C_TRI + P], picked, start=True, stop=True)
                mm = pe.matmul(dst[:, 64:64 + 16 * nt], cst[:, C_ONE:C_ONE + 1].to_broadcast([P, P]), picked, start=True, stop=True)
                done(mm, ("cum", l))
                experts(l)
            assert made == ORDER, [(a, b) for a, b in zip(made, ORDER) if a != b][:4]

        @block.scalar
        def _(act):
            def release(ins, key):
                ins.then_inc(read_sem(key), 1)

            def norm_stats(ready, base, got, sq_sem, var_sem, std_sem, t, scratch):
                act.wait_ge(ready, got)
                act.activation(scratch, x_res[:, t, :], ACT.Square, accum_out=stat[:, base + t:base + t + 1]
                               ).then_inc(sq_sem, 1)
                act.wait_ge(var_sem, t + 1)
                act.activation(stat[:, base + 8 + t:base + 9 + t], stat[:, base + 4 + t:base + 5 + t], ACT.Sqrt
                               ).then_inc(std_sem, 1)

            act.wait_ge(cond_in, 32)
            act.activation(csil[:, :, :, :], cond[:, :, :].unsqueeze(2).to_broadcast([P, KD, 16, 2]), ACT.Silu).then_inc(csil_ready, 1)
            for l in range(LAYERS):
                nt = query_tiles(l)
                nq = nt * P

                def stats(t):
                    if l == 0:
                        norm_stats(x_in if t < XT else ctx_in, 0, 16, ssq[l], var[l], std[l], t, h_tok[:, t, :])
                    else:
                        norm_stats(x_out[0], 0, t + 1, ssq[l], var[l], std[l], t, h_tok[:, t, :])

                def modulated(t):
                    key = ("tr1", l, t, 0)
                    full(act, key)
                    for k in range(4):
                        c = modcol[:, l, 0 if t < XT else 1, :]
                        ins = act.activation(h_t[:, k, t * P:(t + 1) * P], ps(key)[:, k * P:(k + 1) * P], ACT.Identity,
                                             bias=c[:, k:k + 1], scale=c[:, KD + k:KD + k + 1])
                    release(ins, key)

                def squares(t):
                    key = ("F", l, t)
                    lo = 0 if t < nt else 384
                    full(act, key)
                    act.activation(h_tok[:, t, 512 + lo:1024], ps(key)[:, lo:512], ACT.Square).then_inc(fsq[l], 1)
                    act.wait_ge(fvar[l], t + 1)
                    act.activation(fstat[:, 1, lo // 64:8], fstat[:, 0, lo // 64:8], ACT.Sqrt).then_inc(fstd[l], 1)

                stats(0)
                stats(1)
                emptied(act, ("modT", l))
                modulated(0)
                modulated(1)
                if l == 0:
                    act.wait_ge(lam_dots, 1)
                    act.activation(stat[:, 72:76], stat[:, 68:72], ACT.Exp).then_inc(lam_exp, 1)
                for t in range(2, TILES):
                    stats(t)
                    squares(t - 2)
                    modulated(t)
                for t in range(2, TILES):
                    squares(t)
                for kind in ("Ft", "A", "Dt"):
                    if kind == "A":
                        for t in range(XT, TILES):
                            key = ("D", l, t)
                            lo = 0 if t < nt else 256
                            full(act, ("Ft", l, t))
                            full(act, key)
                            act.copy(h_tok[:, t, lo:512], ps(key)[:, lo:512]).then_inc(ctx_copied[l], 1)
                            act.wait_ge(ctx_copied[l], t - XT + 1)
                            act.sem_inc(read_sem(key), 1)
                        for m in range(3):
                            key = ("A", l, m)
                            full(act, key)
                            release(act.mul(qk[:, Q_NA + m, 0:nq], ps(key)[:, 0:nq], 64 ** -0.5), key)
                        continue
                    n_q, q0, k0, scale = (3, Q_GQ, K_GQ, 64 ** -0.5) if kind == "Ft" else (2, Q_DF, K_DF, 32 ** -0.5)
                    for t in range(TILES):
                        key = (kind, l, t)
                        full(act, key)
                        v = ps(key)[:, :].rearrange("p (c t) -> p c t", c=4)
                        if t < nt:
                            act.mul(qk[:, q0:q0 + n_q, t * P:(t + 1) * P], v[:, 0:n_q, :], scale)
                        release(act.copy(qk[:, k0:k0 + 4 - n_q, t * P:(t + 1) * P], v[:, n_q:4, :]), key)
                units = head_units(l)

                def exps(u):
                    kind, h, x = units[u]
                    if u >= 1 and (kind == "diff" or units[u - 1][0] == "diff"):
                        full(act, ("T", l, u - 1, 1 if units[u - 1][2] else 0))
                    if u >= 2:
                        full(act, ("T", l, u - 2, 1 if units[u - 2][2] else 0))
                    if u == 0:
                        full(act, ("Dt", l, TILES - 1))
                    for s in range(2 if kind == "diff" else 1):
                        act.wait_ge(max_ready[l], maxes(l, u, s))
                        buf = s if kind == "diff" else u % 2
                        for q in range(2):
                            n = 2 * buf + q
                            b = ps(("S", l, u, s, q if x else 0))
                            src = b[:, 0:N_TOK] if x else b[:, q * CTX:(q + 1) * CTX]
                            act.activation(prob[buf][:, q, 0:N_TOK if x else CTX], src, ACT.Exp,
                                           bias=stat[:, 48 + n:49 + n], accum_out=stat[:, 52 + n:53 + n]
                                           ).then_inc(exp_ready[l], 1)

                def out_t(u):
                    kind, h, x = units[u]
                    key = ("O", l, u)
                    if kind == "diff":
                        return
                    full(act, key)
                    half = mix_half(kind, h)
                    q0 = 0 if x else SEQ
                    release(act.copy(mixed[64 * half:64 * half + 64, mix_chunk(kind, h), q0:q0 + SEQ],
                                     ps(key)[64 * half:64 * half + 64, 0:SEQ]), key)

                exps(0)
                for u in range(len(units) + 1):
                    if u + 1 < len(units):
                        exps(u + 1)
                    if u < len(units):
                        if units[u][2]:
                            key = ("T", l, u, 1)
                            if u >= 2:
                                full(act, ("O", l, u - 2))
                            full(act, key)
                            release(act.copy(prob_t[u % 2][:, :, P:2 * P],
                                             ps(key)[:, :].rearrange("p (k q) -> p k q", k=4)), key)
                    if u >= 1:
                        out_t(u - 1)
                    if u == sub_norm_unit(l) - 2:
                        act.wait_ge(sub_var[l], 1)
                        act.activation(stat[:, 16:16 + 4 * nt], stat[:, 0:4 * nt], ACT.Sqrt).then_inc(sub_std[l], 1)
                    if u == sub_norm_unit(l):
                        for pair in range(nt // 2):
                            key = ("OBt", l, pair)
                            full(act, key)
                            release(act.copy(mixed[:, 3:5, 2 * pair * P:2 * (pair + 1) * P]
                                             .rearrange("p k (t q) -> p t k q", t=2),
                                             ps(key)[:, :].rearrange("p (t k q) -> p t k q", t=2, k=2)), key)
                for t in range(nt + 1):
                    if t < nt:
                        norm_stats(x_mid[l], 0, t + 1, ssq2[l], var2[l], std2[l], t, h_tok[:, t, :])
                    if t >= 1:
                        for half in range(2):
                            key = ("tr2", l, t - 1, half)
                            full(act, key)
                            release(act.copy(h_t[:, 4 * half:4 * half + 4, (t - 1) * P:t * P],
                                             ps(key)[:, :].rearrange("p (k t) -> p k t", k=4)), key)
                act.wait_ge(gexp_in[l], 1)
                act.activation(rt[:, R_GE:R_GE + 4 * nt], rt[:, R_GD:R_GD + 4 * nt], ACT.Exp).then_inc(gexp[l], 1)
                act.wait_ge(gexp_in[l], 2)
                act.activation(rt[:, R_E2:R_E2 + nt], rt[:, R_DM:R_DM + nt], ACT.Exp).then_inc(gexp[l], 1)
                act.wait_ge(routed[l], 1)
                n_all = act.value_load(counts_i[0:1, 3 * N_EXP:3 * N_EXP + 1], min_val=1, max_val=MAX_BLOCKS)

                act.wait_ge(hgt_full[l], 1)
                act.copy(hgt[:, :, :], bank[0][:, :].rearrange("p (k r) -> p k r", k=KD)).then_inc(hgt_ready[l], 1)
                with act.Fori(0, n_all) as g:
                    for half in range(2):
                        act.wait_ge(gu_full[l], 2 * g + (half + 1))
                        act.activation(sg[0:BLOCK, 256 * half:256 * half + 256], bank[(1, 4)[half]][0:BLOCK, 0:256],
                                       ACT.Silu).then_inc(sg_ready[l], 1)
                    act.wait_ge(hgt_full[l], g + 2)
                    act.copy(hgt[:, :, :], bank[0][:, :].rearrange("p (k r) -> p k r", k=KD)).then_inc(hgt_ready[l], 1)
            for t in range(XT):
                norm_stats(x_out[LAYERS - 1], 32, t + 1, fssq, fin_var, fin_std, t, h_tok[:, t, :])

        @block.vector
        def _(dve):
            chain = [0]

            def link(ins):
                chain[0] += 1
                ins.then_inc(dve_order, 1)
                dve.wait_ge(dve_order, chain[0])

            def release(ins, key):
                ins.then_inc(read_sem(key), 1)

            def norm(l, base, t, sq_sem, var_sem, std_sem, a_row, s_row, dst):
                dve.wait_ge(sq_sem, t + 1)
                dve.tensor_scalar(stat[:, base + 4 + t:base + 5 + t], stat[:, base + t:base + t + 1], 1.0 / D, EPS,
                                  ALU.mult, ALU.add).then_inc(var_sem, 1)
                dve.wait_ge(std_sem, t + 1)
                link(dve.reciprocal(stat[:, base + 12 + t:base + 13 + t], stat[:, base + 8 + t:base + 9 + t]))
                if a_row is None:
                    return dve.tensor_scalar(dst, x_res[:, t, :], stat[:, base + 12 + t:base + 13 + t], None, ALU.mult)
                ins = dve.scalar_tensor_tensor(dst, x_res[:, t, :], stat[:, base + 12 + t:base + 13 + t], a_row,
                                               ALU.mult, ALU.mult)
                if s_row is not None:
                    link(ins)
                    ins = dve.tensor_tensor(dst, dst, s_row, ALU.add)
                return ins

            def mod_rows(l, r, n):
                key = ("mod", l, r)
                full(dve, key)
                gain = mod_add
                if n == 0:
                    dve.wait_ge(mod_first_in, 32)
                    gain = rows[:, 2, 0:512]
                else:
                    dve.wait_ge(mod_b_in, 16 * mod_loads(n, 0))
                    if ROUNDS[n - 1][1] == 0:
                        full(dve, ("modT", ROUNDS[n - 1][0]))
                    else:
                        dve.wait_ge(mod_stored, 32 * mod_stores(n))
                dve.tensor_tensor(mod_row, bank[7][:, :], mod_add, ALU.add).then_inc(mod_sum, 1)
                dve.wait_ge(mod_sum, n + 1)
                dve.sem_inc(read_sem(key), 1)
                if r != 1:
                    rows_p = slice(64, 128) if r == 0 else slice(0, 64)
                    if n >= 1:
                        dve.wait_ge(mod_b_in, 16 * mod_loads(n, 1))
                    dve.scalar_tensor_tensor(mod_row[rows_p, :], mod_row[rows_p, :], 1.0, gain[rows_p, :],
                                             ALU.add, ALU.mult).then_inc(mod_done, 1)
                else:
                    dve.sem_inc(mod_done, 1)

            def mods(at):
                for l, r, k in mod_pieces_after(at):
                    if (r, k) == (1, 0) and l > 0:
                        mod_columns(l)
                    if k == 3:
                        mod_rows(l, r, ROUNDS.index((l, r)))

            def mod_columns(l):
                key = ("modT", l)
                full(dve, key)
                turned_rows = ps(key)[:, :].rearrange("p (m j x) -> p m j x", m=4, j=4)
                for c in range(2):
                    ins = dve.tensor_copy(modcol[:, l, c, :].rearrange("p (j m) -> p m j", m=4), turned_rows[:, :, :, c])
                release(ins, key)
                emptied(dve, key)

            def rope(dst, src, tmp, groups, dim, cc, ss):
                v = src.rearrange("p (g d) -> p g d", d=dim)
                o_ = dst.rearrange("p (g d) -> p g d", d=dim)
                t_ = tmp.rearrange("p (g d) -> p g d", d=dim)
                h = dim // 2
                cb = cc.unsqueeze(1).to_broadcast([P, groups, dim])
                s1 = ss[:, 0:h].unsqueeze(1).to_broadcast([P, groups, h])
                s2 = ss[:, h:dim].unsqueeze(1).to_broadcast([P, groups, h])
                dve.tensor_tensor(o_, v, cb, ALU.mult)
                dve.tensor_tensor(t_[:, :, 0:h], v[:, :, h:dim], s1, ALU.mult)
                link(dve.tensor_tensor(t_[:, :, h:dim], v[:, :, 0:h], s2, ALU.mult))

            dve.memset(zeros[:, :], 0.0).then_inc(zeroed, 1)

            def lambdas():
                dve.wait_ge(consts_in, 16 * N_CONST)
                lq = lam_in[:, 0:256].rearrange("p (v l d) -> p v l d", v=4, l=LAYERS)
                pr = lam_in[:, 256:384].rearrange("p (v l d) -> p v l d", v=2, l=LAYERS)
                for i in range(2):
                    ins = dve.tensor_tensor(pr[:, i], lq[:, 2 * i], lq[:, 2 * i + 1], ALU.mult)
                link(ins)
                dve.tensor_reduce(stat[:, 68:72], lam_in[:, 256:384].rearrange("p (a d) -> p a d", d=32), AX.X,
                                  ALU.add).then_inc(lam_dots, 1)
                dve.wait_ge(lam_exp, 1)
                for l in range(LAYERS):
                    lam_init = 0.8 - 0.6 * math.exp(-0.3 * l)
                    link(dve.tensor_tensor(neglam[:, l:l + 1], stat[:, 74 + l:75 + l], stat[:, 72 + l:73 + l],
                                           ALU.subtract))
                    link(dve.tensor_scalar(neglam[:, l:l + 1], neglam[:, l:l + 1], -lam_init, None, ALU.add))
                    link(dve.tensor_scalar(subg[:, l, :], subg[:, l, :], 1.0 - lam_init, None, ALU.mult))

            def combine(l, t):
                if t == 0:
                    dve.wait_ge(gates_in[l], 16 * 2 * (query_tiles(l) // 2))
                y1, y2 = y_in[t % 2]
                dve.wait_ge(y_back[t % 2][l], 32 * (t // 2 + 1))
                link(dve.tensor_scalar(y1, y1, wsel[:, 0, t:t + 1], None, ALU.mult))
                link(dve.scalar_tensor_tensor(y1, y2, wsel[:, 1, t:t + 1], y1, ALU.mult, ALU.add))
                link(dve.tensor_tensor(y1, y1, rows[:, 0 if t < XT else 1, :], ALU.mult))
                dve.tensor_tensor(x_res[:, t, :], x_res[:, t, :], y1, ALU.add).then_inc(x_out[l], 1)

            for l in range(LAYERS):
                nt = query_tiles(l)

                def first_norm(t):
                    if l > 0:
                        combine(l - 1, t)
                    norm(l, 0, t, ssq[l], var[l], std[l], None, None, h_tok[:, t, :]).then_inc(h_ready[l], 1)

                def modulated(t):
                    key = ("tr1", l, t, 1)
                    full(dve, key)
                    for k in range(4):
                        c = modcol[:, l, 0 if t < XT else 1, 4 + k:5 + k]
                        a_ = modcol[:, l, 0 if t < XT else 1, KD + 4 + k:KD + 5 + k]
                        ins = dve.tensor_scalar(h_t[:, 4 + k, t * P:(t + 1) * P], ps(key)[:, k * P:(k + 1) * P],
                                                a_, c, ALU.mult, ALU.add)
                    release(ins, key)

                n_in = [0]

                def after_in():
                    if l == 0:
                        mods(("in", n_in[0]))
                    n_in[0] += 1

                def gqa_rows(t):
                    key = ("F", l, t)
                    q_heads = 6 if t < nt else 0
                    g0 = 6 - q_heads
                    lo = 64 * g0
                    b = ps(key)
                    hi_ = h_tok[:, t, 512 + lo:1024]
                    lo_ = h_tok[:, t, lo:512]
                    dve.wait_ge(fsq[l], t + 1)
                    link(dve.tensor_reduce(fstat[:, 2, g0:8], hi_.rearrange("p (g d) -> p g d", d=64), AX.X, ALU.add))
                    dve.tensor_scalar(fstat[:, 0, g0:8], fstat[:, 2, g0:8], 1.0 / 64, EPS, ALU.mult,
                                      ALU.add).then_inc(fvar[l], 1)
                    dve.wait_ge(fstd[l], t + 1)
                    link(dve.reciprocal(fstat[:, 2, g0:8], fstat[:, 1, g0:8]))
                    link(dve.tensor_tensor(hi_.rearrange("p (g d) -> p g d", d=64),
                                           b[:, lo:512].rearrange("p (g d) -> p g d", d=64),
                                           fstat[:, 2, g0:8].unsqueeze(2).to_broadcast([P, 8 - g0, 64]), ALU.mult))
                    dst = b if t < XT else h_tok[:, t, :]
                    if q_heads:
                        dve.tensor_tensor(dst[:, 0:384].rearrange("p (m h d) -> p h m d", m=3, h=2),
                                          h_tok[:, t, 512:896].rearrange("p (h m d) -> p h m d", m=3, h=2),
                                          gains[:, l, 0, :].unsqueeze(1).unsqueeze(1).to_broadcast([P, 2, 3, 64]),
                                          ALU.mult)
                    ins = dve.tensor_tensor(dst[:, 384:512].rearrange("p (g d) -> p g d", d=64),
                                            h_tok[:, t, 896:1024].rearrange("p (g d) -> p g d", d=64),
                                            gains[:, l, 1, :].unsqueeze(1).to_broadcast([P, 2, 64]), ALU.mult)
                    if t < XT:
                        link(ins)
                        rope(lo_, b[:, 0:512], hi_, 8, 64, cst[:, C_C32 + 64 * t:C_C32 + 64 * t + 64],
                             cst[:, C_S32 + 64 * t:C_S32 + 64 * t + 64])
                        dve.tensor_tensor(lo_, lo_, hi_, ALU.add).then_inc(rope_ready[l], 1)
                    else:
                        ins.then_inc(rope_ready[l], 1)
                    dve.wait_ge(rope_ready[l], t + 1)
                    dve.sem_inc(read_sem(key), 1)
                    after_in()
                first_norm(0)
                first_norm(1)
                if l == 0:
                    mod_rows(0, 0, 0)
                    mod_columns(0)
                modulated(0)
                modulated(1)
                if l == 0:
                    lambdas()
                for t in range(2, TILES):
                    first_norm(t)
                    gqa_rows(t - 2)
                    modulated(t)
                for t in range(2, TILES):
                    gqa_rows(t)
                for t in range(TILES):
                    if t < XT:
                        key = ("D", l, t)
                        full(dve, ("Ft", l, t))
                        full(dve, key)
                        lo_, hi_ = h_tok[:, t, 0:512], h_tok[:, t, 512:1024]
                        rope(lo_, ps(key)[:, 0:512], hi_, 16, 32, cst[:, C_C16 + 32 * t:C_C16 + 32 * t + 32],
                             cst[:, C_S16 + 32 * t:C_S16 + 32 * t + 32])
                        dve.tensor_tensor(lo_, lo_, hi_, ALU.add).then_inc(rope_ready[l], 1)
                        dve.wait_ge(rope_ready[l], TILES + t + 1)
                        dve.sem_inc(read_sem(key), 1)
                    after_in()
                dve.wait_ge(ga_in[2][l], 64)
                dve.tensor_tensor(rows[:, 0:3, :].rearrange("p a b -> p (a b)").rearrange("p (g c) -> p g c", c=64),
                                  rows[:, 0:3, :].rearrange("p a b -> p (a b)").rearrange("p (g c) -> p g c", c=64),
                                  cst[:, C_MASK:C_MASK + 64].unsqueeze(1).to_broadcast([P, 48, 64]),
                                  ALU.add).then_inc(win_ready[l], 1)
                for p in in_products(l)[2 * TILES:]:
                    if p[0] == "B":
                        full(dve, p)
                        release(dve.tensor_copy(qk[:, K_NA + p[2], :], ps(p)[:, :]), p)
                    elif p[0] == "C":
                        full(dve, p)
                        release(dve.tensor_copy(v_tok[:, p[2], 0:384], ps(p)[:, 0:384]), p)
                    elif p[0] == "E":
                        full(dve, p)
                        release(dve.tensor_copy(v_tok[:, p[2], 384:768], ps(p)[:, 0:384]), p)
                    after_in()
                units = head_units(l)

                def maxima(u):
                    kind, h, x = units[u]
                    for s in range(2 if kind == "diff" else 1):
                        buf = s if kind == "diff" else u % 2
                        for q in range(2):
                            k_ = ("S", l, u, s, q if x else 0)
                            full(dve, k_)
                            src = ps(k_)[:, 0:N_TOK] if x else ps(k_)[:, q * CTX:(q + 1) * CTX]
                            ins = dve.tensor_reduce(stat[:, 48 + 2 * buf + q:49 + 2 * buf + q], src, AX.X, ALU.max,
                                                    negate=True)
                        ins.then_inc(max_ready[l], 1)

                def exp_count(u):
                    return sum(4 if k == "diff" else 2 for k, _, _ in units[:u + 1])

                def normalise(u):
                    kind, h, x = units[u]
                    n_k = N_TOK if x else CTX
                    dve.wait_ge(exp_ready[l], exp_count(u))
                    for s in range(2 if kind == "diff" else 1):
                        for q in range(2 if x else 1):
                            dve.sem_inc(read_sem(("S", l, u, s, q)), 1)
                    if kind == "diff":
                        link(dve.reciprocal(stat[:, 56:60], stat[:, 52:56]))
                        link(dve.tensor_scalar(stat[:, 58:60], stat[:, 58:60], neglam[:, l:l + 1], None, ALU.mult))
                        for q in range(2):
                            ins = dve.tensor_scalar(prob[1][:, q, 0:n_k], prob[1][:, q, 0:n_k],
                                                    stat[:, 58 + q:59 + q], None, ALU.mult)
                        link(ins)
                        for q in range(2):
                            ins = dve.scalar_tensor_tensor(prob[0][:, q, 0:n_k], prob[0][:, q, 0:n_k],
                                                           stat[:, 56 + q:57 + q], prob[1][:, q, 0:n_k],
                                                           ALU.mult, ALU.add)
                    else:
                        n = 2 * (u % 2)
                        link(dve.reciprocal(stat[:, 56 + n:58 + n], stat[:, 52 + n:54 + n]))
                        for q in range(2):
                            ins = dve.tensor_scalar(prob[u % 2][:, q, 0:n_k], prob[u % 2][:, q, 0:n_k],
                                                    stat[:, 56 + n + q:57 + n + q], None, ALU.mult)
                    ins.then_inc(probs_ready[l], 1)

                def turned(u):
                    kind, h, x = units[u]
                    key = ("T", l, u, 0)
                    if u >= 2:
                        full(dve, ("O", l, u - 2))
                    full(dve, key)
                    if x:
                        release(dve.tensor_copy(prob_t[u % 2][:, :, 0:P],
                                                ps(key)[:, :].rearrange("p (k q) -> p k q", k=4)), key)
                    else:
                        release(dve.tensor_copy(prob_t[u % 2][:, 0:2, :],
                                                ps(key)[:, :].rearrange("p (k q) -> p k q", k=2)), key)

                def out_rows(u):
                    kind, h, x = units[u]
                    if kind == "diff":
                        key = ("O", l, u)
                        full(dve, key)
                        t0 = 0 if x else XT
                        release(dve.tensor_copy(ob[:, t0:t0 + 2, 64 * h:64 * h + 64],
                                                ps(key)[:, 0:128].rearrange("p (q d) -> p q d", q=2)), key)

                def sub_norm():
                    emptied(dve, ("O", l, max(u for u, (k, _, _) in enumerate(units) if k == "diff")))
                    sq = ob_sq[:, 0:256 * nt]
                    obv = big[:, 0:256 * nt]
                    link(dve.tensor_tensor(sq, obv, obv, ALU.mult))
                    link(dve.tensor_reduce(stat[:, 32:32 + 4 * nt], sq.rearrange("p (g d) -> p g d", d=64), AX.X, ALU.add))
                    dve.tensor_scalar(stat[:, 0:4 * nt], stat[:, 32:32 + 4 * nt], 1.0 / 64, EPS, ALU.mult,
                                      ALU.add).then_inc(sub_var[l], 1)
                    dve.wait_ge(sub_std[l], 1)
                    link(dve.reciprocal(stat[:, 32:32 + 4 * nt], stat[:, 16:16 + 4 * nt]))
                    og = obv.rearrange("p (g d) -> p g d", d=64)
                    link(dve.tensor_tensor(og, og, stat[:, 32:32 + 4 * nt].unsqueeze(2).to_broadcast([P, 4 * nt, 64]),
                                           ALU.mult))
                    dve.tensor_tensor(og, og, subg[:, l, :].unsqueeze(1).to_broadcast([P, 4 * nt, 64]),
                                      ALU.mult).then_inc(sub_ready[l], 1)

                maxima(0)
                for u in range(len(units) + 1):
                    if u < len(units):
                        normalise(u)
                    if u + 1 < len(units):
                        maxima(u + 1)
                    if u < len(units):
                        turned(u)
                    if u >= 1:
                        out_rows(u - 1)
                    if u == sub_norm_unit(l) - 2:
                        sub_norm()
                    if l == 0:
                        mods(("unit", u))
                dve.wait_ge(gates_in[l], 16 * (nt // 2))
                def residual(t):
                    for half in range(2):
                        key = ("Y", l, t, half)
                        cols = slice(512 * half, 512 * half + 512)
                        full(dve, key)
                        ins = dve.tensor_tensor(h_tok[:, t, cols], ps(key)[:, :], rows[:, 0 if t < XT else 1, cols],
                                                ALU.mult)
                        release(ins, key)
                        emptied(dve, key)
                        ins = dve.tensor_tensor(x_res[:, t, cols], x_res[:, t, cols], h_tok[:, t, cols], ALU.add)
                    ins.then_inc(x_mid[l], 1)

                for t in range(nt):
                    residual(t)
                    if t == 0:
                        dve.wait_ge(ga_in[0][l], 32)
                    if t == XT:
                        dve.wait_ge(ga_in[1][l], 32)
                    a_row, s_row = (rows[:, 2, :], rows[:, 3, :]) if t < XT else (next_rows[:, 0, :], next_rows[:, 1, :])
                    norm(l, 0, t, ssq2[l], var2[l], std2[l], a_row, s_row, h_tok[:, t, :]).then_inc(h2_ready[l], 1)

                def r_(c, n):
                    return rt[:, c:c + n]

                def by_tile(c, n):
                    return rt[:, c:c + n * nt].rearrange("p (t n) -> p t n", t=nt)

                def spread(c, n):
                    return rt[:, c:c + nt].unsqueeze(2).to_broadcast([P, nt, n])

                lgv = lg[:, 0:20 * nt].rearrange("p (t n) -> p t n", t=nt)
                key = ("R", l)
                full(dve, key)
                dve.tensor_tensor(lgv, ps(key)[:, 0:20 * nt].rearrange("p (t n) -> p t n", t=nt),
                                  rbias[:, l, :].unsqueeze(1).to_broadcast([P, nt, 20]), ALU.add
                                  ).then_inc(read_sem(key), 1)
                emptied(dve, key)
                link(dve.tensor_reduce(r_(R_GM, nt), lgv[:, :, 0:4], AX.X, ALU.max))
                dve.tensor_tensor(by_tile(R_GD, 4), lgv[:, :, 0:4], spread(R_GM, 4), ALU.subtract).then_inc(gexp_in[l], 1)
                dve.wait_ge(gexp_in[l], 1)
                link(dve.tensor_scalar(r_(R_C4, 4 * nt), r_(R_GD, 4 * nt), 0.0, None, ALU.is_ge))
                ig = cst[:, C_IG:C_IG + 4].unsqueeze(1).to_broadcast([P, nt, 4])
                ie = cst[:, C_IE:C_IE + 16].unsqueeze(1).to_broadcast([P, nt, 16])
                link(dve.tensor_tensor(by_tile(R_C4, 4), by_tile(R_C4, 4), ig, ALU.mult))
                link(dve.tensor_reduce(r_(R_CI, nt), by_tile(R_C4, 4), AX.X, ALU.min))
                link(dve.tensor_tensor(by_tile(R_OG, 4), ig, spread(R_CI, 4), ALU.is_equal))
                link(dve.tensor_scalar(r_(R_PEN, 4 * nt), r_(R_OG, 4 * nt), -1.0, BIG, ALU.add, ALU.mult))
                for t in range(nt):
                    ins = dve.tensor_tensor(r_(R_E1 + 16 * t, 16).rearrange("p (g e) -> p g e", g=4),
                                            lgv[:, t, 4:20].rearrange("p (g e) -> p g e", g=4),
                                            r_(R_PEN + 4 * t, 4).unsqueeze(2).to_broadcast([P, 4, 4]), ALU.add)
                link(ins)

                def first_largest(src, m, idx, hot):
                    link(dve.tensor_reduce(r_(m, nt), by_tile(src, 16), AX.X, ALU.max))
                    link(dve.tensor_tensor(by_tile(R_EQ, 16), by_tile(src, 16), spread(m, 16), ALU.is_equal))
                    link(dve.tensor_tensor(by_tile(R_EQ, 16), by_tile(R_EQ, 16), ie, ALU.mult))
                    link(dve.tensor_reduce(r_(idx, nt), by_tile(R_EQ, 16), AX.X, ALU.min))
                    link(dve.tensor_tensor(by_tile(hot, 16), ie, spread(idx, 16), ALU.is_equal))

                first_largest(R_E1, R_M1, R_I1, R_O1)
                link(dve.scalar_tensor_tensor(r_(R_X, 16 * nt), r_(R_O1, 16 * nt), -BIG, r_(R_E1, 16 * nt), ALU.mult,
                                              ALU.add))
                first_largest(R_X, R_M2, R_I2, R_O2)
                dve.tensor_tensor(r_(R_M, 16 * nt), r_(R_O1, 16 * nt), r_(R_O2, 16 * nt), ALU.add
                                  ).then_inc(pick_ready[l], 1)
                dve.tensor_tensor(r_(R_DM, nt), r_(R_M2, nt), r_(R_M1, nt), ALU.subtract).then_inc(gexp_in[l], 1)
                dve.wait_ge(gexp[l], 1)
                link(dve.tensor_reduce(r_(R_GS, nt), by_tile(R_GE, 4), AX.X, ALU.add))
                link(dve.reciprocal(r_(R_PG, nt), r_(R_GS, nt)))
                dve.wait_ge(gexp[l], 2)
                link(dve.tensor_scalar(r_(R_DEN, nt), r_(R_E2, nt), 1.0, None, ALU.add))
                link(dve.reciprocal(r_(R_R, nt), r_(R_DEN, nt)))
                link(dve.tensor_tensor(wsel[:, 0, 0:nt], r_(R_R, nt), r_(R_PG, nt), ALU.mult))
                link(dve.tensor_tensor(wsel[:, 1, 0:nt], wsel[:, 0, 0:nt], r_(R_E2, nt), ALU.mult))
                key = ("cum", l)
                full(dve, key)
                dve.tensor_copy(r_(R_LOC, 16 * nt), ps(key)[:, 0:16 * nt])
                dve.tensor_copy(r_(R_TOT, 16 * nt), ps(key)[:, 64:64 + 16 * nt]).then_inc(read_sem(key), 1)
                emptied(dve, key)
                dve.tensor_copy(r_(R_POS, 16), r_(R_LOC, 16))
                for t in range(1, nt):
                    dve.tensor_tensor(r_(R_POS + 16 * t, 16), r_(R_LOC + 16 * t, 16), r_(R_TOT + 16 * (t - 1), 16),
                                      ALU.add)
                    link(dve.tensor_tensor(r_(R_TOT + 16 * t, 16), r_(R_TOT + 16 * t, 16), r_(R_TOT + 16 * (t - 1), 16),
                                           ALU.add))
                n_thr = nt * P // BLOCK - 1
                cmp = r_(R_CMP, 16 * n_thr).rearrange("p (e j) -> p e j", e=16)
                link(dve.tensor_tensor(cmp, r_(R_TOT + 16 * (nt - 1), 16).unsqueeze(2).to_broadcast([P, 16, n_thr]),
                                       cst[:, C_THR:C_THR + n_thr].unsqueeze(1).to_broadcast([P, 16, n_thr]),
                                       ALU.is_gt))
                link(dve.tensor_reduce(r_(R_NB, 16), cmp, AX.X, ALU.add))
                link(dve.tensor_scalar(r_(R_NB, 16), r_(R_NB, 16), 1.0, None, ALU.add))
                link(dve.tensor_copy(r_(R_PA, 16), r_(R_NB, 16)))
                a, b = R_PA, R_PB
                for d in (1, 2, 4, 8):
                    dve.tensor_copy(r_(b, d), r_(a, d))
                    link(dve.tensor_tensor(r_(b + d, 16 - d), r_(a + d, 16 - d), r_(a, 16 - d), ALU.add))
                    a, b = b, a
                link(dve.tensor_tensor(r_(b, 16), r_(a, 16), r_(R_NB, 16), ALU.subtract))
                dve.tensor_copy(counts_i[:, 0:16], r_(R_NB, 16))
                dve.tensor_copy(counts_i[:, 16:32], r_(b, 16))
                dve.tensor_copy(counts_i[:, 32:48], r_(a, 16))
                link(dve.tensor_copy(counts_i[:, 48:49], r_(a + 15, 1)))
                link(dve.tensor_scalar(r_(a, 16), r_(b, 16), float(BLOCK), None, ALU.mult))
                link(dve.tensor_tensor(by_tile(R_RP, 16), by_tile(R_POS, 16),
                                       r_(a, 16).unsqueeze(1).to_broadcast([P, nt, 16]), ALU.add))
                for c, hot in enumerate((R_O1, R_O2)):
                    link(dve.tensor_tensor(r_(R_EQ, 16 * nt), r_(R_RP, 16 * nt), r_(hot, 16 * nt), ALU.mult))
                    link(dve.tensor_reduce(r_(R_ROW + 4 * c, nt), by_tile(R_EQ, 16), AX.X, ALU.add))
                for c in range(2):
                    ins = dve.tensor_copy(route_i[:, 4 * c:4 * c + nt], r_(R_ROW + 4 * c, nt))
                ins.then_inc(routed[l], 1)

                dve.wait_ge(routed[l], 1)
                n_all = dve.value_load(counts_i[0:1, 3 * N_EXP:3 * N_EXP + 1], min_val=1, max_val=MAX_BLOCKS)
                dve.wait_ge(hg_in[l], 16)
                dve.tensor_copy(hg[0:BLOCK, :], hg_ring[0:BLOCK, 0:D]).then_inc(hg_ready[l], 1)
                with dve.Fori(0, n_all) as g:
                    dve.wait_ge(hgt_full[l], g + 1)
                    dve.wait_ge(hg_in[l], 16 * (g + 2))
                    dve.sem_inc(dve_steps, 1)
                    dve.tensor_copy(hg[0:BLOCK, :], hg_ring[0:BLOCK, bass.ds(((g + 1) % HG_AHEAD) * D, D)]
                                    ).then_inc(hg_ready[l], 1)
                    for half in range(2):
                        cols = slice(256 * half, 256 * half + 256)
                        dve.wait_ge(sg_ready[l], 2 * g + (half + 1))
                        dve.tensor_tensor(hid[0:BLOCK, cols], sg[0:BLOCK, cols],
                                          bank[(1, 4)[half]][BLOCK:2 * BLOCK, 0:256], ALU.mult).then_inc(hid_ready[l], 1)
                        dve.wait_ge(hidt_full[l], 2 * g + (half + 1))
                        dve.tensor_copy(hidt[:, 2 * half:2 * half + 2, :],
                                        bank[(2, 5)[half]][:, 0:128].rearrange("p (k r) -> p k r", k=2)
                                        ).then_inc(hidt_ready[l], 1)
                    dve.wait_ge(y_full[l], g + 1)
                    dve.wait_ge(y_free[l], g + 1)
                    dve.sem_inc(dve_steps, 1)
                    dve.tensor_copy(y_ring[:, bass.ds((g % Y_BUFS) * 512, 512)], bank[3][:, :]).then_inc(y_ready[l], 1)
            for t in range(query_tiles(LAYERS - 1)):
                combine(LAYERS - 1, t)
            dve.wait_ge(fin_in, 16)
            for t in range(XT):
                norm(None, 32, t, fssq, fin_var, fin_std, rows[:, 2, :], None, h_tok[:, t, :]).then_inc(fin_ready, 1)

        @block.gpsimd
        def _(pool):
            def row(src):
                return src.to_broadcast([P, src.shape[1]])

            consts = []
            for i, n in enumerate(("diff_lambda_q1", "diff_lambda_k1", "diff_lambda_q2", "diff_lambda_k2")):
                consts.append((lam_in[:, 64 * i:64 * i + 64], row(io[n].rearrange("(a l) d -> a (l d)", a=1))))
            for i, n in enumerate(("gqa_q_norm", "gqa_k_norm")):
                for l in range(LAYERS):
                    consts.append((gains[:, l, i, :], row(io[n][l:l + 1, :])))
            consts.append((subg[:, :, :].rearrange("p l d -> p (l d)"),
                           row(io["diff_subln"].rearrange("(a l) d -> a (l d)", a=1))))
            for dst, src in consts:
                pool.dma_start(dst, src).then_inc(consts_in, 16)
            with nc.allow_non_contiguous_dma(reason="twenty biases"):
                pool.dma_start(rbias[:, :, 0:4], io["router_group_b"].rearrange("(a l) g -> a l g", a=1)
                               .to_broadcast([P, LAYERS, 4])).then_inc(consts_in, 16)
                pool.dma_start(rbias[:, :, 4:20], io["router_expert_b"].rearrange("(a l) g -> a l g", a=1)
                               .to_broadcast([P, LAYERS, 16])).then_inc(consts_in, 16)

            def mod_round(n):
                l, r = ROUNDS[n]
                pool.wait_ge(mod_done, n)
                pool.dma_start(mod_add, chunk_rows(io["b_mod"][l], r * 2048, (r + 1) * 2048)).then_inc(mod_b_in, 16)
                pool.wait_ge(mod_sum, n + 1)
                if r == 0:
                    pool.dma_start(mod_add[64:128, :], chunk_rows(io["norm_attn"][l], 0, D)).then_inc(mod_b_in, 16)
                if r == 2:
                    pool.dma_start(mod_add[0:64, :], chunk_rows(io["norm_ffn"][l], 0, D)).then_inc(mod_b_in, 16)
                pool.wait_ge(mod_done, n + 1)
                if r == 0:
                    return
                for c in range(2):
                    pool.dma_start(modd[l, c, r * 2048:(r + 1) * 2048].rearrange("(j n) -> j n", j=4),
                                   mod_row[c:P:32, :]).then_inc(mod_stored, 16)
                pool.wait_ge(mod_stored, 32 * mod_stores(n + 1))

            def load_row(dst, l, c, sixth, s):
                pool.dma_start(rows[:, dst, :], row(modd[l, c:c + 1, sixth * D:(sixth + 1) * D])).then_inc(s, 16)

            pool.wait_ge(zeroed, 1)
            flat = wind.rearrange("l r h c -> (l r h c)").rearrange("(p a n) -> p a n", a=2, n=128)
            pool.dma_start(flat, zeros[0:flat.shape[0], :].unsqueeze(1).to_broadcast([flat.shape[0], 2, 128])
                           ).then_inc(wind_zero, 16)
            pool.wait_ge(wind_zero, 16)
            for l in range(LAYERS):
                pool.dma_start(wind[l, :, :, 48:79], io["na_rpb"][l].rearrange("h r c -> r h c")).then_inc(wind_in, 16)
            pool.wait_ge(wind_in, 16 * LAYERS)
            for l in range(LAYERS):
                nt = query_tiles(l)
                if l == 0:
                    pool.wait_ge(mod_done, 1)
                    pool.wait_ge(lam_dots, 1)
                else:
                    pool.wait_ge(x_out[l - 1], query_tiles(l - 1))
                for q in range(2):
                    for half in range(2):
                        r = 2 * q + half
                        a = wind[l, 7 - r:11 - r, :, :]
                        src = bass.AP(a.tensor, a.offset, [[1, 64], [128, 24], [1, 64]])
                        pool.dma_start(win[64 * half:64 * half + 64, q, :, :, :].rearrange("p r h c -> p (r h) c"),
                                       src).then_inc(ga_in[2][l], 16)
                if l == 0:
                    for n in range(1, 6):
                        mod_round(n)
                units = head_units(l)
                last_na = max(u for u, (k, _, _) in enumerate(units) if k == "na")
                full(pool, ("T", l, last_na, 0))
                load_row(0, l, 0, 2, gates_in[l])
                if nt > XT:
                    load_row(1, l, 1, 2, gates_in[l])
                load_row(2, l, 0, 4, ga_in[0][l])
                load_row(3, l, 0, 3, ga_in[0][l])
                full(pool, ("OBt", l, nt // 2 - 1))
                if nt > XT:
                    for i, sixth in enumerate((4, 3)):
                        pool.dma_start(next_rows[:, i, :], row(modd[l, 1:2, sixth * D:(sixth + 1) * D])
                                       ).then_inc(ga_in[1][l], 16)
                pool.dma_start(w_route[:, :, 0:4], io["router_group_w"][l].rearrange("(k p) n -> p k n", p=P)
                               ).then_inc(route_w_in[l], 16)
                pool.dma_start(w_route[:, :, 4:20], io["router_expert_w"][l].rearrange("(k p) n -> p k n", p=P)
                               ).then_inc(route_w_in[l], 16)
                pool.wait_ge(x_mid[l], nt)
                load_row(0, l, 0, 5, gates_in[l])
                if nt > XT:
                    load_row(1, l, 1, 5, gates_in[l])
                pool.wait_ge(h2_ready[l], XT)
                if l + 1 == LAYERS:
                    pool.dma_start(rows[:, 2, :], row(io["final_norm"].rearrange("(a d) -> a d", a=1))
                                   ).then_inc(fin_in, 16)
                pool.wait_ge(hbuf_zero, 16)
                pool.wait_ge(routed[l], 1)
                for t in range(nt):
                    for c in range(2):
                        pool.indirect_dma_start(
                            out=hbuf, out_offset=bass.IndirectOffsetOnAxis(ap=route_i[:, 4 * c + t:4 * c + t + 1], axis=0),
                            in_=h_tok[:, t, :], in_offset=None).then_inc(scattered[l], 16)
                pool.wait_ge(scattered[l], 32 * nt)
                for g in range(HG_AHEAD):
                    if g:
                        pool.wait_ge(hg_in[l], 16 * g)
                    pool.dma_start(hg_ring[0:BLOCK, g * D:(g + 1) * D], hbuf[g * BLOCK:(g + 1) * BLOCK, :]
                                   ).then_inc(hg_in[l], 16)
                pool.sem_inc(y_free[l], Y_BUFS)
                n_all = pool.value_load(counts_i[0:1, 3 * N_EXP:3 * N_EXP + 1], min_val=1, max_val=MAX_BLOCKS)
                with pool.Fori(0, n_all) as g:
                    pool.wait_ge(y_ready[l], g + 1)
                    for half in range(2):
                        pool.dma_start(hbuf[bass.ds(g * BLOCK, BLOCK), 512 * half:512 * half + 512],
                                       y_ring[64 * half:64 * half + 64, bass.ds((g % Y_BUFS) * 512, 512)]
                                       ).then_inc(y_stored[l], 16)
                    pool.wait_ge(hg_in[l], 16 * (g + HG_AHEAD))
                    pool.dma_start(hg_ring[0:BLOCK, bass.ds((g % HG_AHEAD) * D, D)],
                                   hbuf[bass.ds((g + HG_AHEAD) * BLOCK, BLOCK), :]).then_inc(hg_in[l], 16)
                    pool.wait_ge(y_stored[l], 32 * (g + 1))
                    pool.sem_inc(y_free[l], 1)
                pool.wait_ge(hg_in[l], 16 * (n_all + HG_AHEAD))
                pool.wait_ge(y_stored[l], 32 * n_all)
                pool.sem_inc(pool_steps, 1)
                for t in range(nt):
                    if t >= 2:
                        pool.wait_ge(x_out[l], t - 1)
                    for c in range(2):
                        pool.indirect_dma_start(
                            out=y_in[t % 2][c], out_offset=None, in_=hbuf,
                            in_offset=bass.IndirectOffsetOnAxis(ap=route_i[:, 4 * c + t:4 * c + t + 1], axis=0)
                        ).then_inc(y_back[t % 2][l], 16)
            for t in range(XT):
                pool.wait_ge(fin_ready, t + 1)
                pool.dma_start(out[0, t * P:(t + 1) * P, :], h_tok[:, t, :]).then_inc(stored, 16)
            pool.wait_ge(stored, 16 * XT)


_INS = ["x", "c", "ctx", "c_ctx", "w_mod", "b_mod", "norm_attn", "norm_ffn", "w_in", "w_out", "na_rpb",
        "diff_lambda_q1", "diff_lambda_k1", "diff_lambda_q2", "diff_lambda_k2", "diff_subln", "gqa_q_norm",
        "gqa_k_norm", "router_group_w", "router_group_b", "router_expert_w", "router_expert_b", "w_gate", "w_up",
        "w_down", "final_norm"]


def kernel(**inputs):
    import numpy as _np
    import concourse.bacc as _bacc
    from concourse import mybir as _mybir
    from concourse.bass_utils import run_bass_kernel_spmd as _run

    nc = _bacc.Bacc("TRN2", target_bir_lowering=False, num_devices=1)
    arrays, io = {}, {}
    for name in _INS + ["consts"]:
        a = constant_table() if name == "consts" else _np.ascontiguousarray(inputs[name])
        arrays[f"in_{name}_dram"] = a
        io[name] = nc.dram_tensor(f"in_{name}_dram", a.shape, _mybir.dt.from_np(a.dtype), kind="ExternalInput").ap()
    out = nc.dram_tensor("out_0_dram", (1, SEQ, D), _mybir.dt.float32, kind="ExternalOutput").ap()
    hybrid_block(nc, io, out)
    r = _run(nc, [arrays], core_ids=[0])
    return r.results[0]["out_0_dram"]
```
